# Optimizing a Trainium2 kernel written in Bass

```python
import jax, jax.numpy as jnp
from jax import lax
import numpy as np
import math
import jax
import jax.numpy as jnp

D_MODEL = 1024
BATCH = 1
SEQ = 256
DEPTH = 1

N_HEADS_ATTN = 8
HEAD_DIM = 64
ATTN_WIDTH = N_HEADS_ATTN * HEAD_DIM
IDX_HEADS = 8
IDX_DIM = 32
TOPK_MAX = 256
Q_BLOCK = 128
CONV_WIDTH = D_MODEL - ATTN_WIDTH
CONV_GROUPS = 8
CONV_K = 3
MIX_WIDTH = ATTN_WIDTH + CONV_WIDTH
ROPE_THETA = 500000.0
ROPE_DIM = HEAD_DIM // 4
D_FF = ((-(-8 * D_MODEL // 3)) + 255) // 256 * 256
DEEPNORM_ALPHA = (2.0 * DEPTH) ** 0.25
DEEPNORM_BETA = (8.0 * DEPTH) ** -0.25
EPS = 1e-5
NEG_INF = -1e30

IN_SPLITS = (ATTN_WIDTH, HEAD_DIM, HEAD_DIM, IDX_HEADS * IDX_DIM, IDX_DIM, IDX_HEADS,
             CONV_WIDTH, CONV_WIDTH, CONV_WIDTH)
IN_COLS = sum(IN_SPLITS)


def rope_tables(seq_len):
    pos = jnp.arange(seq_len, dtype=jnp.float32)
    inv = ROPE_THETA ** (-(jnp.arange(0, ROPE_DIM, 2, dtype=jnp.float32) / ROPE_DIM))
    ang = pos[:, None] * inv[None, :]
    return jnp.cos(ang)[:, None, :], jnp.sin(ang)[:, None, :]

def partial_rope(x, cos, sin):
    cos = cos.astype(x.dtype)
    sin = sin.astype(x.dtype)
    half = ROPE_DIM // 2
    x1, x2, rest = x[..., :half], x[..., half:ROPE_DIM], x[..., ROPE_DIM:]
    return jnp.concatenate([x1 * cos - x2 * sin, x2 * cos + x1 * sin, rest], axis=-1)

def layer_norm(x, g, b):
    xf = x.astype(jnp.float32)
    mu = jnp.mean(xf, axis=-1, keepdims=True)
    var = jnp.mean(jnp.square(xf - mu), axis=-1, keepdims=True)
    y = (xf - mu) * lax.rsqrt(var + EPS) * g.astype(jnp.float32) + b.astype(jnp.float32)
    return y.astype(x.dtype)

def group_rms_norm(x, g, n_groups):
    bsz, s, w = x.shape
    xf = x.astype(jnp.float32).reshape(bsz, s, n_groups, w // n_groups)
    xf = xf * lax.rsqrt(jnp.mean(jnp.square(xf), axis=-1, keepdims=True) + EPS)
    return (xf.reshape(bsz, s, w) * g.astype(jnp.float32)).astype(x.dtype)

def modulate(x, shift, scale):
    return x * (1.0 + scale[:, None, :]) + shift[:, None, :]

def sparse_indexer_attention(q, k, v, qi, ki, wi, k_sel):
    bsz, s, h, dh = q.shape
    n_blk = s // Q_BLOCK
    attn_scale = HEAD_DIM ** -0.5
    key_pos = jnp.arange(s)
    ki32 = ki.astype(jnp.float32)

    def to_blocks(a):
        return jnp.moveaxis(a.reshape((bsz, n_blk, Q_BLOCK) + a.shape[2:]), 1, 0)

    def block_fn(args):
        q_b, qi_b, w_b, t_b = args
        rel = jax.nn.relu(jnp.einsum('bqhd,bsd->bqhs', qi_b.astype(jnp.float32), ki32))
        score = jnp.einsum('bqhs,bqh->bqs', rel, w_b.astype(jnp.float32))
        causal = key_pos[None, :] <= t_b[:, None]
        score = jnp.where(causal[None], score, NEG_INF)
        _, sel = lax.top_k(score, k_sel)
        valid = sel <= t_b[None, :, None]
        kg = jax.vmap(lambda kb, ib: kb[ib])(k, sel)
        vg = jax.vmap(lambda vb, ib: vb[ib])(v, sel)
        logits = jnp.einsum('bqhd,bqkd->bhqk', q_b, kg).astype(jnp.float32) * attn_scale
        logits = jnp.where(valid[:, None], logits, NEG_INF)
        p = jax.nn.softmax(logits, axis=-1).astype(v.dtype)
        return jnp.einsum('bhqk,bqkd->bqhd', p, vg)

    t_blocks = key_pos.reshape(n_blk, Q_BLOCK)
    out = lax.map(block_fn, (to_blocks(q), to_blocks(qi), to_blocks(wi), t_blocks))
    return jnp.moveaxis(out, 0, 1).reshape(bsz, s, h, dh)

def token_mixer(h, w_in, conv_w, attn_norm_g, conv_norm_g, w_out, cos, sin):
    bsz, s, _ = h.shape
    k_sel = min(TOPK_MAX, s // 4)
    proj = h @ w_in
    offsets = np.cumsum(IN_SPLITS)[:-1].tolist()
    q, k, v, qi, ki, wi, gate_b, gate_c, hc = jnp.split(proj, offsets, axis=-1)

    q = partial_rope(q.reshape(bsz, s, N_HEADS_ATTN, HEAD_DIM), cos, sin)
    k = partial_rope(k[:, :, None, :], cos, sin)[:, :, 0, :]
    qi = partial_rope(qi.reshape(bsz, s, IDX_HEADS, IDX_DIM), cos, sin)
    ki = partial_rope(ki[:, :, None, :], cos, sin)[:, :, 0, :]
    wi = wi * (IDX_HEADS ** -0.5 * IDX_DIM ** -0.5)
    attn = sparse_indexer_attention(q, k, v, qi, ki, wi, k_sel).reshape(bsz, s, ATTN_WIDTH)
    attn = group_rms_norm(attn, attn_norm_g, N_HEADS_ATTN)

    u = gate_c * hc
    u_pad = jnp.pad(u, ((0, 0), (CONV_K - 1, 0), (0, 0)))
    conv = sum(conv_w[j] * u_pad[:, j:j + s, :] for j in range(CONV_K))
    conv_out = group_rms_norm(gate_b * conv, conv_norm_g, CONV_GROUPS)

    mixed = jnp.concatenate([attn, conv_out], axis=-1)
    return mixed @ w_out

def swiglu(h, w_gate, w_up, w_down):
    return (jax.nn.silu(h @ w_gate) * (h @ w_up)) @ w_down

def first_inputs(seed: int = 0) -> dict:
    key = jax.random.key(seed)
    ks = jax.random.split(key, 17)
    n = jax.random.normal
    f32 = jnp.float32
    L = DEPTH
    return {
        "x": n(ks[0], (BATCH, SEQ, D_MODEL), f32),
        "c": n(ks[1], (BATCH, D_MODEL), f32),
        "w_ada": n(ks[2], (L, D_MODEL, 6 * D_MODEL), f32) * (D_MODEL ** -0.5),
        "b_ada": n(ks[3], (L, 6 * D_MODEL), f32) * 0.02,
        "w_in": n(ks[4], (L, D_MODEL, IN_COLS), f32) * (D_MODEL ** -0.5),
        "conv_w": n(ks[5], (L, CONV_K, CONV_WIDTH), f32) * (CONV_K ** -0.5),
        "attn_norm_g": 1.0 + 0.1 * n(ks[6], (L, ATTN_WIDTH), f32),
        "conv_norm_g": 1.0 + 0.1 * n(ks[7], (L, CONV_WIDTH), f32),
        "w_out": n(ks[8], (L, MIX_WIDTH, D_MODEL), f32) * (MIX_WIDTH ** -0.5) * DEEPNORM_BETA,
        "ln1_g": 1.0 + 0.1 * n(ks[9], (L, D_MODEL), f32),
        "ln1_b": 0.02 * n(ks[10], (L, D_MODEL), f32),
        "w_gate": n(ks[11], (L, D_MODEL, D_FF), f32) * (D_MODEL ** -0.5),
        "w_up": n(ks[12], (L, D_MODEL, D_FF), f32) * (D_MODEL ** -0.5),
        "w_down": n(ks[13], (L, D_FF, D_MODEL), f32) * (D_FF ** -0.5) * DEEPNORM_BETA,
        "ln2_g": 1.0 + 0.1 * n(ks[14], (L, D_MODEL), f32),
        "ln2_b": 0.02 * n(ks[15], (L, D_MODEL), f32),
    }

def first_block(x, c, w_ada, b_ada, w_in, conv_w, attn_norm_g, conv_norm_g, w_out,
              ln1_g, ln1_b, w_gate, w_up, w_down, ln2_g, ln2_b):
    s = x.shape[1]
    cos, sin = rope_tables(s)
    c_act = jax.nn.silu(c)
    for l in range(DEPTH):
        mod = c_act @ w_ada[l] + b_ada[l]
        sh1, sc1, g1, sh2, sc2, g2 = jnp.split(mod, 6, axis=-1)
        mix = token_mixer(modulate(x, sh1, sc1), w_in[l], conv_w[l], attn_norm_g[l],
                          conv_norm_g[l], w_out[l], cos, sin)
        x = layer_norm(DEEPNORM_ALPHA * x + g1[:, None, :] * mix, ln1_g[l], ln1_b[l])
        ff = swiglu(modulate(x, sh2, sc2), w_gate[l], w_up[l], w_down[l])
        x = layer_norm(DEEPNORM_ALPHA * x + g2[:, None, :] * ff, ln2_g[l], ln2_b[l])
    return x


DEPTH_2 = 2

N_MIXERS = 2
N_SUBLAYERS = 3
ATTN_HEADS = 8
ATTN_HEAD_DIM = D_MODEL // (2 * ATTN_HEADS)
ATTN_V_DIM = 2 * ATTN_HEAD_DIM
NUM_BUCKETS = 32
MAX_DISTANCE = 128
HGRN_EXPAND = 128
HGRN_HEADS = D_MODEL // HGRN_EXPAND
HGRN_FORGET_DIM = HGRN_HEADS * HGRN_EXPAND
HGRN_HEAD_V = D_MODEL // HGRN_HEADS
HGRN_CHUNK = 64
D_FF_2 = 2816
N_ATTN_LAYERS = (DEPTH_2 + 1) // 2
N_HGRN_LAYERS = DEPTH_2 // 2
EPS_2 = 1e-6


def rms_norm(h, gain):
    h32 = h.astype(jnp.float32)
    h32 = h32 * lax.rsqrt(jnp.mean(h32 * h32, axis=-1, keepdims=True) + EPS_2)
    return (h32 * gain.astype(jnp.float32)).astype(h.dtype)

def t5_causal_bucket(dist):
    max_exact = NUM_BUCKETS // 2
    d = jnp.maximum(dist, 0)
    d_f = jnp.maximum(d, 1).astype(jnp.float32)
    large = max_exact + (jnp.log(d_f / max_exact) / math.log(MAX_DISTANCE / max_exact)
                         * (NUM_BUCKETS - max_exact)).astype(jnp.int32)
    large = jnp.minimum(large, NUM_BUCKETS - 1)
    return jnp.where(d < max_exact, d, large)

def swiglu_2(h, w_in, w_down):
    a, b = jnp.split(h @ w_in, 2, axis=-1)
    return (jax.nn.silu(a) * b) @ w_down

def diff_attention(h, w_qkv, w_o, q_gain, k_gain, lam, subln_gain, rel_bias, layer_idx):
    B, S, _ = h.shape
    H, hd, dv = ATTN_HEADS, ATTN_HEAD_DIM, ATTN_V_DIM
    q, k, v = jnp.split(h @ w_qkv, 3, axis=-1)
    q = rms_norm(q.reshape(B, S, H, 2, hd), q_gain) * (hd ** -0.5)
    k = rms_norm(k.reshape(B, S, H, 2, hd), k_gain)
    v = v.reshape(B, S, H, dv)
    lambda_init = 0.8 - 0.6 * math.exp(-0.3 * layer_idx)
    lam32 = lam.astype(jnp.float32)
    lam_full = (jnp.exp(jnp.sum(lam32[0] * lam32[1])) - jnp.exp(jnp.sum(lam32[2] * lam32[3]))
                + lambda_init)
    kt = k.transpose(0, 2, 3, 1, 4)
    vt = v.transpose(0, 2, 1, 3)
    nb = S // Q_BLOCK
    qb = q.reshape(B, nb, Q_BLOCK, H, 2, hd).transpose(1, 0, 3, 4, 2, 5)
    k_pos = jnp.arange(S)

    def block(args):
        q_blk, blk = args
        q_pos = blk * Q_BLOCK + jnp.arange(Q_BLOCK)
        dist = q_pos[:, None] - k_pos[None, :]
        bias = rel_bias[t5_causal_bucket(dist)].astype(jnp.float32).transpose(2, 0, 1)
        s = jnp.einsum('bhcqd,bhckd->bhcqk', q_blk, kt).astype(jnp.float32) + bias[None, :, None]
        s = jnp.where(dist >= 0, s, -jnp.inf)
        p = jax.nn.softmax(s, axis=-1)
        a = p[:, :, 0] - lam_full * p[:, :, 1]
        return jnp.einsum('bhqk,bhkv->bhqv', a, vt)

    o = lax.map(block, (qb, jnp.arange(nb)))
    o = o.transpose(1, 0, 3, 2, 4).reshape(B, S, H, dv)
    o = rms_norm(o, subln_gain) * (1.0 - lambda_init)
    return o.reshape(B, S, H * dv).astype(h.dtype) @ w_o

def hgrn2(h, w_in, w_o, out_gain, lb):
    B, S, _ = h.shape
    H, dk, dv, C = HGRN_HEADS, HGRN_EXPAND, HGRN_HEAD_V, HGRN_CHUNK
    F = HGRN_FORGET_DIM
    q, f, i, g = jnp.split(h @ w_in, [F, 2 * F, 2 * F + D_MODEL], axis=-1)
    f32 = f.astype(jnp.float32)
    lb32 = lb.astype(jnp.float32)
    log_forget = jnp.logaddexp(jnp.log(lb32), jnp.log1p(-lb32) + jax.nn.log_sigmoid(f32))
    k = (1.0 - lb32) * jax.nn.sigmoid(-f32)
    nc = S // C

    def to_chunks(t, d):
        return t.astype(jnp.float32).reshape(B, nc, C, H, d).transpose(1, 0, 3, 2, 4)

    qs, ks, gs = to_chunks(q, dk), to_chunks(k, dk), to_chunks(log_forget, dk)
    vs = to_chunks(i, dv)
    causal = jnp.tril(jnp.ones((C, C), dtype=bool))[None, None, :, :, None]

    def step(state, inp):
        qc, kc, vc, gc = inp
        G = jnp.cumsum(gc, axis=2)
        o_inter = jnp.einsum('bhtk,bhkv->bhtv', qc * jnp.exp(G), state)
        diff = G[:, :, :, None, :] - G[:, :, None, :, :]
        decay = jnp.exp(jnp.where(causal, diff, -jnp.inf))
        scores = jnp.einsum('bhtk,bhsk,bhtsk->bhts', qc, kc, decay)
        o_intra = jnp.einsum('bhts,bhsv->bhtv', scores, vc)
        G_last = G[:, :, -1:, :]
        new_state = (jnp.exp(G_last[:, :, 0, :])[..., None] * state
                     + jnp.einsum('bhsk,bhsv->bhkv', kc * jnp.exp(G_last - G), vc))
        return new_state, o_inter + o_intra

    state0 = jnp.zeros((B, H, dk, dv), jnp.float32)
    _, o = lax.scan(step, state0, (qs, ks, vs, gs))
    o = o.transpose(1, 0, 3, 2, 4).reshape(B, S, H, dv)
    o = rms_norm(o, out_gain.reshape(H, dv)) * jax.nn.silu(g.astype(jnp.float32)).reshape(B, S, H, dv)
    return o.reshape(B, S, D_MODEL).astype(h.dtype) @ w_o

def _normal(key, shape, scale):
    return jax.random.normal(key, shape, jnp.float32) * scale

def second_inputs(seed: int = 0) -> dict:
    key = jax.random.key(seed)
    ks = jax.random.split(key, 20)
    D, F2 = D_MODEL, 2 * HGRN_FORGET_DIM + 2 * D_MODEL
    return {
        'x': _normal(ks[0], (BATCH, SEQ, D), 1.0),
        'c': _normal(ks[1], (BATCH, D), 1.0),
        'ada_w': _normal(ks[2], (DEPTH_2, D, N_SUBLAYERS * 3 * D), 0.5 * D ** -0.5),
        'ada_b': _normal(ks[3], (DEPTH_2, N_SUBLAYERS * 3 * D), 0.02),
        'norm_g': 1.0 + _normal(ks[4], (DEPTH_2, N_SUBLAYERS, D), 0.02),
        'ffn_w_in': _normal(ks[5], (DEPTH_2, 2, D, 2 * D_FF_2), D ** -0.5),
        'ffn_w_down': _normal(ks[6], (DEPTH_2, 2, D_FF_2, D), D_FF_2 ** -0.5),
        'attn_w_qkv': _normal(ks[7], (N_ATTN_LAYERS, D, 3 * D), D ** -0.5),
        'attn_w_o': _normal(ks[8], (N_ATTN_LAYERS, D, D), D ** -0.5),
        'attn_q_gain': 1.0 + _normal(ks[9], (N_ATTN_LAYERS, ATTN_HEAD_DIM), 0.02),
        'attn_k_gain': 1.0 + _normal(ks[10], (N_ATTN_LAYERS, ATTN_HEAD_DIM), 0.02),
        'attn_lambda': _normal(ks[11], (N_ATTN_LAYERS, 4, ATTN_HEAD_DIM), 0.1),
        'attn_subln_gain': 1.0 + _normal(ks[12], (N_ATTN_LAYERS, ATTN_V_DIM), 0.02),
        'rel_bias': _normal(ks[13], (NUM_BUCKETS, ATTN_HEADS), 0.5),
        'hgrn_w_in': _normal(ks[14], (N_HGRN_LAYERS, D, F2), D ** -0.5),
        'hgrn_w_o': _normal(ks[15], (N_HGRN_LAYERS, D, D), D ** -0.5),
        'hgrn_out_gain': 1.0 + _normal(ks[16], (N_HGRN_LAYERS, D), 0.02),
        'hgrn_lb_logits': _normal(ks[17], (N_HGRN_LAYERS, HGRN_FORGET_DIM), 0.1),
    }

def second_block(x, c, ada_w, ada_b, norm_g, ffn_w_in, ffn_w_down, attn_w_qkv, attn_w_o,
              attn_q_gain, attn_k_gain, attn_lambda, attn_subln_gain, rel_bias,
              hgrn_w_in, hgrn_w_o, hgrn_out_gain, hgrn_lb_logits):
    B = x.shape[0]
    lb_all = jnp.cumsum(jax.nn.softmax(hgrn_lb_logits.astype(jnp.float32), axis=0), axis=0)
    lb_all = lb_all - lb_all[0:1]
    c_act = jax.nn.silu(c)
    for layer in range(DEPTH_2):
        mod = (c_act @ ada_w[layer] + ada_b[layer]).reshape(B, N_SUBLAYERS, 3, D_MODEL)
        shift = mod[:, :, 0][:, None]
        scale = mod[:, :, 1][:, None]
        gate = mod[:, :, 2][:, None]
        h = rms_norm(x, norm_g[layer, 0]) * (1.0 + scale[:, :, 0]) + shift[:, :, 0]
        x = x + 0.5 * gate[:, :, 0] * swiglu_2(h, ffn_w_in[layer, 0], ffn_w_down[layer, 0])
        h = rms_norm(x, norm_g[layer, 1]) * (1.0 + scale[:, :, 1]) + shift[:, :, 1]
        j = layer // N_MIXERS
        if layer % N_MIXERS == 0:
            y = diff_attention(h, attn_w_qkv[j], attn_w_o[j], attn_q_gain[j], attn_k_gain[j],
                               attn_lambda[j], attn_subln_gain[j], rel_bias, layer)
        else:
            y = hgrn2(h, hgrn_w_in[j], hgrn_w_o[j], hgrn_out_gain[j], lb_all[j])
        x = x + gate[:, :, 1] * y
        h = rms_norm(x, norm_g[layer, 2]) * (1.0 + scale[:, :, 2]) + shift[:, :, 2]
        x = x + 0.5 * gate[:, :, 2] * swiglu_2(h, ffn_w_in[layer, 1], ffn_w_down[layer, 1])
    return x


def setup_inputs(seed=0):
    out = dict(first_inputs(seed))
    for name, value in second_inputs(seed + 1).items():
        if name != "x":
            out[name + "_2"] = value
    return out


def reference(
    x, c, w_ada, b_ada, w_in, conv_w, attn_norm_g, conv_norm_g, w_out, ln1_g, ln1_b, w_gate,
    w_up, w_down, ln2_g, ln2_b, c_2, ada_w_2, ada_b_2, norm_g_2, ffn_w_in_2, ffn_w_down_2,
    attn_w_qkv_2, attn_w_o_2, attn_q_gain_2, attn_k_gain_2, attn_lambda_2, attn_subln_gain_2,
    rel_bias_2, hgrn_w_in_2, hgrn_w_o_2, hgrn_out_gain_2, hgrn_lb_logits_2,
):
    x = first_block(
        x, c, w_ada, b_ada, w_in, conv_w, attn_norm_g, conv_norm_g, w_out, ln1_g, ln1_b, w_gate,
        w_up, w_down, ln2_g, ln2_b,
    )
    return second_block(
        x, c_2, ada_w_2, ada_b_2, norm_g_2, ffn_w_in_2, ffn_w_down_2, attn_w_qkv_2, attn_w_o_2,
        attn_q_gain_2, attn_k_gain_2, attn_lambda_2, attn_subln_gain_2, rel_bias_2, hgrn_w_in_2,
        hgrn_w_o_2, hgrn_out_gain_2, hgrn_lb_logits_2,
    )


_drawn_inputs = setup_inputs


def setup_inputs(seed=0):
    import zlib

    import numpy as np

    out = dict(_drawn_inputs(seed))
    spreads = {}
    factors = {'norm_g_2': 4.769,
     'attn_q_gain_2': 8.0,
     'attn_k_gain_2': 8.0,
     'attn_lambda_2': 3.936,
     'attn_subln_gain_2': 8.0,
     'hgrn_out_gain_2': 8.0}
    for name, (base, spread) in spreads.items():
        noise = np.random.default_rng([zlib.crc32(name.encode()), seed]).standard_normal(out[name].shape)
        drawn = base * np.exp(spread * noise) if base else spread * noise
        out[name] = jnp.asarray(drawn.astype(out[name].dtype))
    for name, factor in factors.items():
        out[name] = (out[name] * factor).astype(out[name].dtype)
    return out
```

```python
import math
from contextlib import ExitStack

import concourse.bass as bass
import numpy as np
from concourse import mybir

F32 = mybir.dt.float32
F32R = mybir.dt.float32r
U8 = mybir.dt.uint8
ALU = mybir.AluOpType
ACT = mybir.ActivationFunctionType
AX = mybir.AxisListType

P = 128
TOK = 256
NT = TOK // P
D = 1024
KT = D // P
FF = 2816
FC = 256
NCH = FF // FC
BANK = 512
UNIT = 2048
RING = 3
NSUB = 8
HEADS = 8
ALPHA = 2.0 ** 0.25
EPS1, EPS2 = 1e-5, 1e-6
NEG = -1e30
AW = 512
TOKC = 936
KO, VO, QIO, KIO, WIO = 512, 576, 640, 896, 928
TOPK = 64
IDX_SCALE = 8 ** -0.5 * 32 ** -0.5
BUCKETS = 32
LAMBDA_INIT = 0.8 - 0.6 * math.exp(0.0)
TOE = 384
CHUNK = 64
LEVELS = (64, 32, 16, 8, 4, 2, 1)

V_C, V_C2, V_NORM, V_AG, V_CG, V_CW, V_OG, V_LB, V_QG, V_KG, V_SG = 0, 8, 16, 64, 68, 72, 84, 92, 100, 101, 102
NVEC = 103
PRE = KT
UNITS = (14, 33, 33, 16, 33, 33, 20, 33)
FIRST = tuple(PRE + sum(UNITS[:s]) for s in range(NSUB + 1))
SWIGLUS = (1, 2, 4, 5, 7)
SUMS = {0: 5, 1: 2, 3: 10, 6: 2}
LN_ROOT, ATT_ROOT, QK_ROOT = {0: 3, 1: 5}, {0: 1, 3: 19, 6: 27}, 11
RMS_ROOT = {1: 7, 2: 9, 3: 21, 4: 23, 5: 25, 6: 29}
COL_BANK = 7
HGRN_BLOCKS = (1024, 1536, 0, 512, 2048, 2560, 3072, 3584)
AHEAD = {0: (1,), 1: (2,), 2: (3, 4), 4: (5,), 5: (6, 7)}


def sums_before(s):
    return sum(n for k, n in SUMS.items() if k < s)


def GATE_BANK(s):
    return 4 if s else 2


def shape_constants():
    f = np.float32
    ident = np.eye(P, dtype=f)
    q, k = np.arange(P)[:, None], np.arange(TOK)[None, :]
    causal = np.where(k > q + P, f(NEG), f(0)).astype(f)
    inv = f(500000.0) ** (-(np.arange(0, 16, 2, dtype=f) / f(16)))
    ang = np.arange(TOK, dtype=f)[:, None] * inv[None, :].astype(f)
    cos = np.cos(ang).astype(f).reshape(NT, P, 8).transpose(1, 0, 2).reshape(P, 16)
    sin = np.sin(ang).astype(f).reshape(NT, P, 8).transpose(1, 0, 2).reshape(P, 16)
    half = (np.arange(P)[:, None] // 64 == np.arange(2)[None, :]).astype(f)
    consts = np.concatenate([ident, causal, cos, sin, half], axis=1)
    spread = (np.arange(8)[:, None] == (np.arange(AW)[None, :] // 64)).astype(f)
    dist = 255 - np.arange(TOE)
    d_f = np.maximum(dist, 1).astype(f)
    large = 16 + (np.log(d_f / f(16)) / f(math.log(128 / 16)) * f(16)).astype(np.int32)
    bucket = np.where(dist < 16, np.maximum(dist, 0), np.minimum(large, BUCKETS - 1))
    bucket = np.where(dist < 0, BUCKETS, bucket)
    onehot = (np.arange(BUCKETS + 1)[:, None] == bucket[None, :]).astype(f)
    s, t = np.arange(P)[:, None], np.arange(P)[None, :]
    masks = [s == t] + [(s // (2 * n) == t // (2 * n)) & (s % (2 * n) < n) & (t % (2 * n) >= n) for n in LEVELS]
    return consts, spread, onehot, np.stack(masks, 1).astype(np.uint8)


C_ID, C_CAUSAL, C_COS, C_SIN, C_HALF, C_END = 0, 128, 384, 400, 416, 418


def two_blocks(
    nc, x, c, w_ada, b_ada, w_in, conv_w, attn_norm_g, conv_norm_g, w_out, ln1_g, ln1_b, w_gate,
    w_up, w_down, ln2_g, ln2_b, c_2, ada_w_2, ada_b_2, norm_g_2, ffn_w_in_2, ffn_w_down_2,
    attn_w_qkv_2, attn_w_o_2, attn_q_gain_2, attn_k_gain_2, attn_lambda_2, attn_subln_gain_2,
    rel_bias_2, hgrn_w_in_2, hgrn_w_o_2, hgrn_out_gain_2, hgrn_lb_logits_2, out, last=NSUB - 1,
):
    consts, spread, onehot, masks = (
        nc.inline_tensor(a, name=n).ap() for a, n in
        zip(shape_constants(), ("shape_consts", "group_spread", "bucket_onehot", "level_masks")))
    bias_rows = nc.dram_tensor("bias_rows", (P, HEADS, TOE), F32, kind="Internal").ap()
    run_ahead = {s: tuple(a for a in v if a <= last) for s, v in AHEAD.items()}

    def ada_weight(s):
        w = w_ada[0] if s < 2 else ada_w_2[(s - 2) // 3]
        first = (s if s < 2 else (s - 2) % 3) * 3 * D
        return w, first

    def ada_bias(s):
        b = b_ada[0:1] if s < 2 else ada_b_2[(s - 2) // 3:(s - 2) // 3 + 1]
        first = (s if s < 2 else (s - 2) % 3) * 3 * D
        return b[:, first:first + 3 * D]

    def swiglu_weights(s):
        if s == 1:
            return w_gate[0], w_up[0], w_down[0]
        layer, which = ((0, 0), (0, 1), (1, 0), (1, 1))[(2, 4, 5, 7).index(s)]
        w = ffn_w_in_2[layer, which]
        return w[:, 0:FF], w[:, FF:2 * FF], ffn_w_down_2[layer, which]

    with ExitStack() as ctx:
        def sb(name, shape, dt=F32):
            return ctx.enter_context(nc.sbuf_tensor(name, shape, dt))

        def sem(name):
            return ctx.enter_context(nc.semaphore(name))

        raw = sb("raw", [P, RING, UNIT])
        whi = sb("whi", [P, RING, UNIT], F32R)
        wlo = sb("wlo", [P, RING, UNIT], F32R)
        ada_raw = sb("ada_raw", [P, 3, D])
        ada_acc = sb("ada_acc", [P, 2, 3 * D])
        xs = sb("xs", [P, NT, D])
        xn = sb("xn", [P, NT, D])
        hf = sb("hf", [P, KT, TOK])
        hhi = sb("hhi", [P, KT, TOK], F32R)
        hlo = sb("hlo", [P, KT, TOK], F32R)
        gate = sb("gate", [P, 2, D])
        act = sb("act", [P, NT, FC])
        ahi = sb("ahi", [P, 2, TOK], F32R)
        alo = sb("alo", [P, 2, TOK], F32R)
        big = sb("big", [P, 10240])
        kc = sb("kc", [P, C_END])
        ones = sb("ones", [P, P])
        vec = sb("vec", [P, NVEC])
        csil = sb("csil", [P, 16])
        modc = sb("modc", [P, 2, 16])
        mask8 = sb("mask8", [P, len(LEVELS) + 1, P], U8)
        st = sb("st", [P, 256])
        ps = ctx.enter_context(nc.psum_tensor("ps", [P, 8, BANK], F32))
        psf = ps[:, :, :].rearrange("p b n -> p (b n)")

        ident = kc[:, C_ID:C_ID + P]
        half = st[:, 240:241]

        lam_rows = gate[:, 1, BANK:BANK + 256]

        qkv = big[:, 0:6144].rearrange("p (t n) -> p t n", t=NT)
        relb = big[:, 6144:8192].rearrange("p (h k) -> p h k", h=HEADS)
        soft = big[:, 8192:9216].rearrange("p (b c k) -> p b c k", b=2, c=2)
        weightsT = big[:, 9216:9728].rearrange("p (b n) -> p b n", b=2)
        qT, kT = xn[:, :, :].rearrange("p t (h n) -> p (t h) n", n=TOK), hf

        def by_head(flat):
            return flat.rearrange("p (h n) -> p h n", h=HEADS)

        h_q, h_k, h_G = (by_head(big[:, 2048 * n:2048 * (n + 1)]) for n in range(3))
        h_v, h_g = (big[:, 6144 + 2048 * n:8192 + 2048 * n].rearrange("p (t n) -> p t n", t=NT) for n in range(2))
        h_o = big[:, 0:2048].rearrange("p (t n) -> p t n", t=NT)
        scoresT = ada_acc[:, 0, :].rearrange("p (b n) -> p b n", n=P)
        chunk_carry = act[:, :, :].rearrange("p t n -> p (t n)")
        lb, one_less_lb = st[:, 224:232], st[:, 232:240]

        def decayed(level):
            return hf[:, :, :] if level % 2 else by_head(xn[:, :, :].rearrange("p t n -> p (t n)"))

        def halves(place, level):
            n = LEVELS[level - 1] if level <= len(LEVELS) else P
            return place.rearrange("p h (b a n) -> p (h b) a n", a=2, n=n)

        def bank(b, n=1):
            return psf[:, b * BANK:(b + n) * BANK]

        w_land = [sem(f"w_land{i}") for i in range(RING)]
        w_hi, w_lo, w_used = sem("w_hi"), sem("w_lo"), sem("w_used")
        a_land = [sem(f"a_land{i}") for i in range(3)]
        a_used = sem("a_used")
        acc_zero, acc_bias = sem("acc_zero"), sem("acc_bias")
        const_land, x_land, vec_land = sem("const_land"), sem("x_land"), sem("vec_land")
        ones_set, vec_tr, vec_set, csil_set = sem("ones_set"), sem("vec_tr"), sem("vec_set"), sem("csil_set")
        cols_sum, cols_set, gate_sum, gate_set = sem("cols_sum"), sem("cols_set"), sem("gate_sum"), sem("gate_set")
        h_src, h_tr, h_mod, h_hi, h_lo = sem("h_src"), sem("h_tr"), sem("h_mod"), sem("h_hi"), sem("h_lo")
        y_ready, x_new, root = sem("y_ready"), sem("x_new"), sem("root")
        gu_ready, silu_done, act_ready = sem("gu_ready"), sem("silu_done"), sem("act_ready")
        tr_ready, ahi_ready, alo_ready = sem("tr_ready"), sem("ahi_ready"), sem("alo_ready")
        mix_f, mix_hi, mix_lo = sem("mix_f"), sem("mix_hi"), sem("mix_lo")
        v_step, p_step, s_step = sem("v_step"), sem("p_step"), sem("s_step")
        ln_land, out_done = sem("ln_land"), sem("out_done")
        spread_land, mask_land, toe_land, lam_land = sem("spread_land"), sem("mask_land"), sem("toe_land"), sem("lam_land")
        sums_s, sums_v, root_in = sem("sums_s"), sem("sums_v"), sem("root_in")
        blk_ready, q_out, hc_out, rope_done, qk_tr = sem("blk_ready"), sem("q_out"), sem("hc_out"), sem("rope_done"), sem("qk_tr")
        qT_out, kT_out, idx_mm, relu_done, score_done = sem("qT_out"), sem("kT_out"), sem("idx_mm"), sem("relu_done"), sem("score_done")
        conv_u, conv_gated, conv_sq, group_mm = sem("conv_u"), sem("conv_gated"), sem("conv_sq"), sem("group_mm")
        group_tr, group_out, spread_mm = sem("group_tr"), sem("group_out"), sem("spread_mm")
        att_mm, max_done, exp_done, p_tr = sem("att_mm"), sem("max_done"), sem("exp_done"), sem("p_tr")
        pt_s, pt_v, pv_mm, o_done, o_tr = sem("pt_s"), sem("pt_v"), sem("pv_mm"), sem("o_done"), sem("o_tr")
        v_out, qk_sq, qk_out, qT3, kT3 = sem("v_out"), sem("qk_sq"), sem("qk_out"), sem("qT3"), sem("kT3")
        lam_dot, lam_exp, gains_set, dot_mm, sm_ready, sm_exp = sem("lam_dot"), sem("lam_exp"), sem("gains_set"), sem("dot_mm"), sem("sm_ready"), sem("sm_exp")
        a_ready, a_tr, aT_out, av_mm, head_sq = sem("a_ready"), sem("a_tr"), sem("aT_out"), sem("av_mm"), sem("head_sq")
        toe_fill, toe_mm, toe_rows, scan_set = sem("toe_fill"), sem("toe_mm"), sem("toe_rows"), sem("scan_set")
        lb_diff, lb_exp, f_log, f_taken, f_exp, k_ready = sem("lb_diff"), sem("lb_exp"), sem("f_log"), sem("f_taken"), sem("f_exp"), sem("k_ready")
        q_copied, vg_out, lv_sub, lv_exp, lv_mul = sem("q_copied"), sem("vg_out"), sem("lv_sub"), sem("lv_exp"), sem("lv_mul")
        lv_mm, lv_copy, g_silu = sem("lv_mm"), sem("lv_copy"), sem("g_silu")

        def linked(engine, own):
            count = [0]

            def link(instruction):
                count[0] += 1
                instruction.then_inc(own, 1)
                engine.wait_ge(own, count[0])
            return link

        def used(unit, lap=0):
            return unit - PRE + 1 + RING * lap

        def ring_view(ring, unit, k):
            return ring[:, unit % RING, :].rearrange("p (k n) -> p k n", k=k)

        def chunk_units(s, i):
            return FIRST[s] + 3 * i - 1 if i else FIRST[s], FIRST[s] + 3 * i if i else FIRST[s] + 1, FIRST[s] + 3 * i + 1

        def down_unit(s, i):
            return FIRST[s] + 3 * i + 4 if i < NCH - 1 else FIRST[s] + UNITS[s] - 1

        def piece_base(s):
            return KT + 3 * KT * (s - 1)

        block = ctx.enter_context(nc.Block())

        @block.sync
        def _(sp):
            def load(unit, parts, lap=0):
                if unit >= RING:
                    sp.wait_ge(w_lo, unit - RING + 1 + RING * lap)
                for dst, src in parts:
                    sp.dma_start(dst, src).then_inc(w_land[unit % RING], 32 // len(parts))

            def rows(w, k0, k, c0, n):
                return w[k0 * P:(k0 + k) * P, c0:c0 + n].rearrange("(k p) n -> p k n", p=P)

            def load_block(unit, w, c0, n=BANK):
                for g in range(2):
                    dst = raw[:, (unit + g) % RING, 0:4 * n].rearrange("p (k n) -> p k n", k=4)
                    load(unit + g, [(dst, rows(w, 4 * g, 4, c0, n))])

            def load_out(unit, w):
                for j in range(4):
                    load(unit + j, [(ring_view(raw, unit + j, 2), rows(w, 2 * j, 2, 0, D))])

            w0, first = ada_weight(0)
            sp.dma_start(kc[:, :], consts[:, :]).then_inc(const_land, 16)
            vrow = big
            for row, src in ((V_C, c), (V_C2, c_2), (V_AG, attn_norm_g), (V_CG, conv_norm_g),
                             (V_OG, hgrn_out_gain_2), (V_LB, hgrn_lb_logits_2)):
                n = src.shape[-1] // P
                sp.dma_start(vrow[row:row + n, 0:P], src.rearrange("a (k p) -> (a k) p", p=P)).then_inc(vec_land, 16)
            sp.dma_start(vrow[V_NORM:V_NORM + 48, 0:P],
                         norm_g_2.rearrange("l s (k p) -> (l s k) p", p=P)).then_inc(vec_land, 16)
            sp.dma_start(vrow[V_CW:V_CW + 12, 0:P],
                         conv_w[0].rearrange("j (k p) -> (j k) p", p=P)).then_inc(vec_land, 16)
            for row, src in ((V_QG, attn_q_gain_2), (V_KG, attn_k_gain_2)):
                for c0 in (0, 64):
                    sp.dma_start(vrow[row:row + 1, c0:c0 + 64], src[:, :]).then_inc(vec_land, 16)
            sp.dma_start(vrow[V_SG:V_SG + 1, 0:P], attn_subln_gain_2[:, :]).then_inc(vec_land, 16)
            for kt in range(KT):
                load(kt, [(raw[:, kt % RING, :], w0[kt * P:(kt + 1) * P, first:first + 2 * D])])
                if kt == 2:
                    for t in range(NT):
                        sp.dma_start(xs[:, t, :], x[0, t * P:(t + 1) * P, :]).then_inc(x_land, 16)
                    sp.dma_start(mask8[:, :, :], masks[:, :, :]).then_inc(mask_land, 16)
                    sp.dma_start(lam_rows, attn_lambda_2.rearrange("a b n -> a (b n)").to_broadcast((P, 256)))\
                        .then_inc(lam_land, 16)

            U = FIRST[0]
            load_block(U, w_in[0], 0)
            load_block(U + 2, w_in[0], BANK, TOKC - BANK)
            for b, c0 in enumerate((TOKC + 2 * AW, TOKC + AW, TOKC)):
                load_block(U + 4 + 2 * b, w_in[0], c0)
            load_out(U + 10, w_out[0])
            sp.wait_ge(vec_tr, 1)
            for n, row in enumerate((ln1_g, ln1_b)):
                sp.dma_start(big[:, n * D:(n + 1) * D], row.to_broadcast((P, D))).then_inc(ln_land, 16)

            def swiglu(s):
                g, u, d = swiglu_weights(s)

                def gate_up(unit, i, g0, lap=0):
                    slot = raw[:, unit % RING, :].rearrange("p (k h n) -> p k h n", k=4, h=2)
                    load(unit, [(slot[:, :, j, :],
                                 w[g0 * 4 * P:(g0 + 1) * 4 * P, bass.ds(i * FC, FC)].rearrange("(k p) n -> p k n", p=P))
                                for j, w in enumerate((g, u))], lap)

                def down(unit, i, lap=0):
                    load(unit, [(ring_view(raw, unit, 2),
                                 d[bass.ds(i * FC, FC), :].rearrange("(k p) n -> p k n", p=P))], lap)

                def body(units, i, lap=0):
                    gate_up(units[0], i, 0, lap)
                    gate_up(units[1], i, 1, lap)
                    down(units[2], i - 1, lap)

                gate_up(FIRST[s], 0, 0)
                gate_up(FIRST[s] + 1, 0, 1)
                body(chunk_units(s, 1), 1)
                with sp.Fori(2, NCH - 1) as i:
                    body(chunk_units(s, 2), i, i - 2)
                body(chunk_units(s, NCH - 1), NCH - 1)
                down(down_unit(s, NCH - 1), NCH - 1)

            for s in range(1, last + 1):
                if s in SWIGLUS:
                    swiglu(s)
                elif s == 3:
                    with sp.Fori(0, 2) as i:
                        for b in range(3):
                            for g in range(2):
                                unit = FIRST[3] + 2 * b + g
                                load(unit, [(ring_view(raw, unit, 4),
                                             attn_w_qkv_2[0][4 * g * P:4 * (g + 1) * P, bass.ds(b * D + i * BANK, BANK)]
                                             .rearrange("(k p) n -> p k n", p=P))], 2 * i)
                    load_out(FIRST[3] + 12, attn_w_o_2[0])
                else:
                    for b, c0 in enumerate(HGRN_BLOCKS):
                        load_block(FIRST[s] + 2 * b, hgrn_w_in_2[0], c0)
                    load_out(FIRST[s] + 16, hgrn_w_o_2[0])
                if s == 1:
                    sp.wait_ge(x_new, 2)
                    for n, row in enumerate((ln2_g, ln2_b)):
                        sp.dma_start(big[:, n * D:(n + 1) * D], row.to_broadcast((P, D))).then_inc(ln_land, 16)
            for t in range(NT):
                sp.wait_ge(x_new, 2 * last + t + 1)
                sp.dma_start(out[0, t * P:(t + 1) * P, :], xs[:, t, :]).then_inc(out_done, 16)
            sp.wait_ge(out_done, 32)

        @block.gpsimd
        def _(pool):
            link = linked(pool, p_step)

            def reciprocal_root(sums, value, col, width, n, eps):
                pool.wait_ge(sums, value)
                cols = st[:, col:col + width]
                pool.tensor_scalar(cols, cols, 1.0 / n, eps, ALU.mult, ALU.add).then_inc(root_in, 1)
                rooted[0] += 1
                pool.wait_ge(root_in, rooted[0])
                pool.tensor_tensor(cols, cols, half.to_broadcast((P, width)), ALU.pow).then_inc(root, 1)

            rooted = [0]

            def start_sums(s):
                if s >= 2:
                    pool.wait_ge(gate_sum, s - 1)
                pool.memset(ada_acc[:, s % 2, :], 0.0).then_inc(acc_zero, 1)
                pool.wait_ge(acc_zero, s + 1)
                pool.dma_start(ada_acc[0:1, s % 2, :], ada_bias(s)).then_inc(acc_bias, 16)

            def ada_pieces(group):
                for s in group:
                    start_sums(s)
                base, m = piece_base(group[0]), len(group)
                with pool.Fori(0, KT) as kt:
                    for g, s in enumerate(group):
                        w, first = ada_weight(s)
                        for j in range(3):
                            n = base + 3 * g + j
                            pool.wait_ge(a_used, n - 2 + 3 * m * kt)
                            pool.dma_start(ada_raw[:, j, :], w[bass.ds(kt * P, P), first + j * D:first + (j + 1) * D])\
                                .then_inc(a_land[j], 16)

            pool.memset(st[:, :], 0.0).then_inc(ones_set, 1)
            pool.wait_ge(ones_set, 1)
            pool.memset(half, -0.5).then_inc(ones_set, 1)
            pool.memset(ones[:, :], 1.0).then_inc(ones_set, 1)
            start_sums(0)
            pool.dma_start(gate[0:8, 1, 0:AW], spread[:, :]).then_inc(spread_land, 16)
            w0, first = ada_weight(0)
            for kt in range(KT):
                if kt:
                    pool.wait_ge(a_used, kt)
                pool.dma_start(ada_raw[:, 2, :], w0[kt * P:(kt + 1) * P, first + 2 * D:first + 3 * D])\
                    .then_inc(a_land[2], 16)

            def rms_roots(s):
                for t in range(NT):
                    reciprocal_root(sums_s, 2 * (s - 1) + t + 1, t, 1, D, EPS2)

            def ln_roots(s):
                for t in range(NT):
                    reciprocal_root(sums_v, sums_before(s) + SUMS[s] - 1 + t, 5 + 2 * t, 1, 1, EPS1)

            for s in range(last + 1):
                if s in run_ahead and run_ahead[s]:
                    if s == 1:
                        pool.wait_ge(x_new, 2)
                        pool.dma_start(big[0:BUCKETS + 1, 2048:2048 + TOE], onehot[:, :]).then_inc(toe_land, 16)
                        pool.memset(big[0:BUCKETS + 1, 2440:2448], NEG).then_inc(toe_fill, 1)
                        pool.wait_ge(toe_fill, 1)
                        pool.dma_start(big[0:BUCKETS, 2440:2448], rel_bias_2[:, :]).then_inc(toe_land, 16)
                        pool.wait_ge(toe_land, 32)
                        pool.tensor_copy(big[0:BUCKETS + 1, 2560:3584].rearrange("b (h q) -> b h q", h=HEADS),
                                         big[0:BUCKETS + 1, 2440:2448].unsqueeze(2).to_broadcast((BUCKETS + 1, HEADS, P)))\
                            .then_inc(toe_fill, 1)
                    ada_pieces(run_ahead[s])
                if s == 0:
                    reciprocal_root(sums_v, 1, 40, 16, 64, EPS1)
                    for t in range(NT):
                        reciprocal_root(sums_v, 2 + t, 120 + 8 * t, 8, 64, EPS1)
                    ln_roots(0)
                elif s == 1:
                    if last >= 3:
                        pool.wait_ge(toe_rows, HEADS)
                        pool.dma_start(bias_rows[:, :, :], big[:, 3584:3584 + HEADS * TOE].rearrange("p (h j) -> p h j", h=HEADS))\
                            .then_inc(toe_land, 16)
                        pool.wait_ge(toe_land, 48)
                        skewed = bass.AP(tensor=bias_rows.tensor, offset=bias_rows.offset + P - 1,
                                         ap=[[HEADS * TOE - 1, P], [TOE, HEADS], [1, TOK]])
                        pool.dma_start(big[:, 6144:8192].rearrange("p (h k) -> p h k", h=HEADS), skewed)\
                            .then_inc(toe_land, 16)
                    ln_roots(1)
                if s == 3:
                    for n in range(8):
                        reciprocal_root(sums_v, sums_before(3) + n + 1, 152 + 8 * (n % 4), 8, 64, EPS2)
                    for t in range(NT):
                        reciprocal_root(sums_v, sums_before(3) + 9 + t, 120 + 8 * t, 8, P, EPS2)
                if s == 6:
                    pool.wait_ge(gate_sum, 7)
                    pool.memset(ada_acc[:, 0, :], 0.0).then_inc(scan_set, 1)
                    pool.wait_ge(w_used, used(FIRST[6] - 1))
                    flat = act[:, :, :].rearrange("p t n -> p (t n)")
                    pool.memset(flat, 1.0).then_inc(scan_set, 1)
                    pool.wait_ge(scan_set, 2)
                    pool.memset(flat[:, 0:2 * TOK:CHUNK], 0.0).then_inc(scan_set, 1)
                    for t in range(NT):
                        reciprocal_root(sums_v, sums_before(6) + 1 + t, 120 + 8 * t, 8, P, EPS2)
                if 1 <= s < last:
                    rms_roots(s)

        @block.scalar
        def _(sc):
            link = linked(sc, s_step)

            def hi(unit, lap=0, n=UNIT):
                slot, fill = unit % RING, unit // RING + 1
                sc.wait_ge(w_land[slot], 32 * fill + 32 * lap)
                if unit - PRE >= RING:
                    sc.wait_ge(w_used, used(unit - RING, lap))
                sc.activation(whi[:, slot, 0:n], raw[:, slot, 0:n], ACT.Copy).then_inc(w_hi, 1)

            def prefetch(s):
                for j in range(2):
                    hi(FIRST[s] + j)

            def split_inputs(s):
                for t in range(NT):
                    for g in range(2):
                        sc.wait_ge(h_mod, 4 * s + 2 * t + g + 1)
                        sc.activation(hhi[:, 4 * g:4 * g + 4, t * P:(t + 1) * P],
                                      hf[:, 4 * g:4 * g + 4, t * P:(t + 1) * P], ACT.Copy).then_inc(h_hi, 1)

            def split_mixed(n, k0, k, t0, tn):
                sc.wait_ge(mix_f, n)
                sc.activation(hhi[:, k0:k0 + k, t0:t0 + tn], hf[:, k0:k0 + k, t0:t0 + tn], ACT.Copy).then_inc(mix_hi, 1)

            def set_gate(s):
                sc.wait_ge(gate_sum, s + 1)
                sc.activation(gate[:, s % 2, :], bank(GATE_BANK(s), 2), ACT.Copy,
                              scale=1.0 if s in (0, 1, 3, 6) else 0.5).then_inc(gate_set, 1)

            def normalise(s):
                for t in range(NT):
                    sc.wait_ge(x_new, 2 * s + t + 1)
                    sc.activation(xn[:, t, :], xs[:, t, :], ACT.Square,
                                  accum_out=st[:, t:t + 1]).then_inc(sums_s, 1)
                    sc.wait_ge(root, RMS_ROOT[s] + t + 1)
                    sc.activation(xn[:, t, :], xs[:, t, :], ACT.Copy, scale=st[:, t:t + 1]).then_inc(h_src, 1)

            def swiglu(s):
                m = SWIGLUS.index(s) * NCH
                U = FIRST[s]

                def silu(i, unit, lap=0):
                    for t in range(NT):
                        if t == 0:
                            sc.wait_ge(gu_ready, m + i + 1)
                        else:
                            sc.wait_ge(w_used, used(unit, lap))
                        sc.activation(act[:, t, :], ps[:, 4 + t, 0:FC], ACT.Silu).then_inc(silu_done, 1)

                def ahi_of(i):
                    sc.wait_ge(tr_ready, m + i + 1)
                    sc.activation(ahi[:, :, :].rearrange("p k n -> p (k n)"), bank(6), ACT.Copy).then_inc(ahi_ready, 1)

                def body(first, i, lap=0, more=True):
                    hi(first + 2, lap)
                    ahi_of(i - 1)
                    if more:
                        hi(first + 3, lap)
                    silu(i, first + 1, lap)
                    if more:
                        hi(first + 4, lap)

                hi(U + 2)
                silu(0, U + 1)
                hi(U + 3)
                body(U + 2, 1)
                if s == 1 and last >= 3:
                    for h in range(HEADS):
                        sc.wait_ge(toe_mm, h + 1)
                        sc.activation(big[:, 3584 + h * TOE:3584 + (h + 1) * TOE], ps[:, 6 + h % 2, 0:TOE], ACT.Copy)\
                            .then_inc(toe_rows, 1)
                with sc.Fori(2, NCH - 1) as i:
                    body(U + 5, i, i - 2)
                body(U + 3 * (NCH - 1) - 1, NCH - 1, more=False)
                hi(U + UNITS[s] - 1)
                ahi_of(NCH - 1)

            def swiglu_end(s):
                if s < last:
                    hi(FIRST[s + 1])
                    set_gate(s + 1)
                    hi(FIRST[s + 1] + 1)
                    normalise(s)

            def attention():
                U = FIRST[3]
                with sc.Fori(0, 2) as i:
                    hi(U + 2, 2 * i)
                    hi(U + 3, 2 * i)
                    for b in range(2):
                        for t in range(NT):
                            if t == 0:
                                sc.wait_ge(blk_ready, 2 + 3 * i + b + 1)
                            else:
                                sc.wait_ge(w_used, used(U + 2 * b + 1, 2 * i))
                            n = 2 * b + t
                            sc.activation(big[:, 8192 + n * BANK:8192 + (n + 1) * BANK], bank(2 * b + t), ACT.Square).then_inc(qk_sq, 1)
                        hi(U + 4 + 2 * b, 2 * i)
                        hi(U + 5 + 2 * b, 2 * i)
                    for t in range(NT):
                        if t == 0:
                            sc.wait_ge(blk_ready, 2 + 3 * i + 3)
                        else:
                            sc.wait_ge(w_used, used(U + 5, 2 * i))
                        sc.activation(qkv[:, t, bass.ds(2 * D + i * BANK, BANK)], bank(4 + t), ACT.Copy).then_inc(v_out, 1)
                    sc.wait_ge(qk_out, 4 * i + 4)
                for t in range(NT):
                    for g in range(2):
                        sc.wait_ge(qk_tr, 2 + 4 * t + 2 * g + 1)
                        sc.activation(qT[:, 4 * g:4 * g + 4, t * P:(t + 1) * P],
                                      bank(4 * t + 2 * g).rearrange("p (h n) -> p h n", h=4), ACT.Copy,
                                      scale=st[:, 216:217]).then_inc(qT3, 1)

                def softmax(i):
                    t, keys = i // HEADS, P * (i // HEADS + 1)
                    sc.wait_ge(sm_ready, i + 1)
                    for c in range(2):
                        p = soft[:, i % 2, c, 0:keys]
                        done = sc.activation(p, p, ACT.Exp, bias=st[:, 88 + 2 * (i % 2) + c:89 + 2 * (i % 2) + c],
                                             accum_out=st[:, 72 + 2 * (i % 2) + c:73 + 2 * (i % 2) + c])
                    done.then_inc(sm_exp, 1)

                def take_weights(i):
                    keys = P * (i // HEADS + 1)
                    sc.wait_ge(a_tr, i + 1)
                    if i >= 2:
                        sc.wait_ge(av_mm, i - 1)
                    sc.activation(weightsT[:, i % 2, 0:keys], ps[:, 4 + i % 2, 0:keys], ACT.Copy).then_inc(aT_out, 1)

                def square_heads(t):
                    sc.wait_ge(av_mm, HEADS * (t + 1))
                    sc.activation(qkv[:, t, D:2 * D], bank(6, 2), ACT.Square).then_inc(head_sq, 1)

                for i in range(2 * HEADS):
                    softmax(i)
                    if i:
                        take_weights(i - 1)
                    if i == HEADS + 2:
                        square_heads(0)
                take_weights(2 * HEADS - 1)
                square_heads(1)
                for t in range(NT):
                    for g in range(2):
                        split_mixed(3 + 2 * t + g + 1, 4 * g, 4, t * P, P)
                if last > 3:
                    set_gate(4)
                hi(U + 14)
                hi(U + 15)
                if last > 3:
                    hi(FIRST[4])
                    hi(FIRST[4] + 1)
                    normalise(3)

            def hgrn():
                U = FIRST[6]
                flat_xn = xn[:, :, :].rearrange("p t n -> p (t n)")

                def forget(b):
                    e0 = flat_xn[:, b * D:(b + 1) * D]
                    sc.wait_ge(w_used, used(U + 2 * b + 1))
                    link(sc.activation(e0, bank(2 * b, 2), ACT.Abs))
                    hi(U + 4 + 3 * b)
                    if b == 0:
                        sc.wait_ge(lb_diff, 1)
                        sc.activation(lb, lb, ACT.Exp).then_inc(lb_exp, 1)
                    link(sc.activation(e0, e0, ACT.Exp, scale=-1.0))
                    sc.activation(e0, e0, ACT.Ln, bias=ones[:, 0:1]).then_inc(f_log, 1)
                    hi(U + 5 + 3 * b)
                    sc.wait_ge(f_taken, b + 1)
                    heads = slice(4 * b, 4 * b + 4)
                    sc.activation(h_k[:, heads, :], h_k[:, heads, :], ACT.Exp)
                    link(sc.activation(hf[:, heads, :], hf[:, heads, :], ACT.Exp, scale=-1.0))
                    sc.wait_ge(lb_diff, 2)
                    for h in range(4 * b, 4 * b + 4):
                        done = sc.activation(hf[:, h, :], hf[:, h, :], ACT.Ln, bias=ones[:, 0:1], scale=lb[:, h:h + 1])
                    done.then_inc(f_exp, 1)

                def take_queries(b):
                    sc.wait_ge(w_used, used(U + 5 + 2 * b))
                    sc.activation(h_q[:, 4 * b:4 * b + 4, :], bank(2 * b, 2).rearrange("p (h n) -> p h n", h=4), ACT.Copy)\
                        .then_inc(q_copied, 1)

                def exps(level):
                    E = decayed(level)
                    sc.wait_ge(lv_sub, level)
                    if level == 1:
                        e, g = halves(E, 1), halves(h_G, 1)
                        sc.activation(e[:, :, 0, :], e[:, :, 0, :], ACT.Exp)
                        done = sc.activation(e[:, :, 1, :], g[:, :, 1, :], ACT.Exp)
                    elif level <= len(LEVELS):
                        done = sc.activation(E, E, ACT.Exp)
                    else:
                        sc.activation(E[:, :, 0:P], E[:, :, 0:P], ACT.Exp)
                        sc.activation(E[:, :, P:P + CHUNK], h_G[:, :, P:P + CHUNK], ACT.Exp)
                        done = sc.activation(E[:, :, P + CHUNK:TOK], E[:, :, P + CHUNK:TOK], ACT.Exp)
                    done.then_inc(lv_exp, 1)

                def take_tokens(b):
                    for t in range(NT):
                        if t == 0:
                            sc.wait_ge(blk_ready, 8 + b + 1)
                        else:
                            sc.wait_ge(w_used, used(U + 9 + 2 * b))
                        dst = (h_v, h_g)[b // 2][:, t, (b % 2) * BANK:(b % 2 + 1) * BANK]
                        sc.activation(dst, bank(2 * (b % 2) + t), ACT.Copy).then_inc(vg_out, 1)

                hi(U + 2)
                hi(U + 3)
                forget(0)
                hi(U + 6)
                forget(1)
                take_queries(0)
                hi(U + 9)
                take_queries(1)
                hi(U + 10)
                for level in range(len(LEVELS) + 2):
                    if level <= 7:
                        hi(U + 11 + level)
                    if level <= len(LEVELS):
                        exps(level + 1)
                    if level % 2 and level <= 7:
                        take_tokens(level // 2)
                sc.wait_ge(vg_out, 8)
                sc.activation(h_g[:, :, :], h_g[:, :, :], ACT.Silu).then_inc(g_silu, 1)
                for t in range(NT):
                    sc.wait_ge(pv_mm, 2 + t + 1)
                    sc.activation(xn[:, t, :], bank(2 * t, 2), ACT.Square).then_inc(head_sq, 1)
                for t in range(NT):
                    for g in range(2):
                        split_mixed(7 + 2 * t + g + 1, 4 * g, 4, t * P, P)
                if last > 6:
                    set_gate(7)
                hi(U + 19)
                if last > 6:
                    hi(FIRST[7])
                    hi(FIRST[7] + 1)
                    normalise(6)

            sc.wait_ge(vec_land, 208)
            sc.wait_ge(vec_set, 1)
            sc.activation(csil[:, :], vec[:, V_C:V_C + 16], ACT.Silu).then_inc(csil_set, 1)
            split_inputs(0)
            U = FIRST[0]
            n_b = 4 * (TOKC - BANK)
            hi(U)
            hi(U + 1)
            hi(U + 2, n=n_b)
            tok = big[:, 2048:2048 + NT * TOKC].rearrange("p (t n) -> p t n", t=NT)
            L = big[:, 3920:5968].rearrange("p (h k) -> p h k", h=HEADS)
            PT = big[:, 5968:8016].rearrange("p (g n) -> p g n", g=2)
            hi(U + 3, n=n_b)
            sc.wait_ge(blk_ready, 1)
            sc.activation(tok[:, 0, 0:BANK], bank(4), ACT.Copy).then_inc(q_out, 1)
            sc.wait_ge(w_used, used(U + 1))
            sc.activation(tok[:, 1, 0:BANK], bank(5), ACT.Copy).then_inc(q_out, 1)
            hi(U + 4)
            hi(U + 5)
            hi(U + 6)
            hi(U + 7)
            sc.wait_ge(w_used, used(U + 5))
            hfl = hf[:, :, :].rearrange("p k n -> p (k n)")
            xfl = xn[:, :, :].rearrange("p t n -> p (t n)")
            sc.wait_ge(h_lo, 4)
            sc.activation(hfl[:, 0:D], bank(0, 2), ACT.Copy).then_inc(hc_out, 1)
            sc.wait_ge(qk_tr, 1)
            sc.activation(xfl[:, 0:D], bank(4, 2), ACT.Copy).then_inc(qT_out, 1)
            hi(U + 8)
            hi(U + 9)
            for t in range(NT):
                keys = P * (t + 1)
                sc.wait_ge(idx_mm, t + 1)
                if t:
                    sc.wait_ge(score_done, t)
                for r in range(4):
                    ins = ps[:, 4 + r, 0:2 * keys].rearrange("p (j k) -> p j k", j=2)
                    outs = L.rearrange("p (j r) k -> p j r k", r=4)[:, :, r, 0:keys]
                    last_op = sc.activation(outs, ins, ACT.Relu)
                    if r == 3:
                        last_op.then_inc(relu_done, 1)
            set_gate(0)
            sc.wait_ge(conv_gated, 1)
            sc.activation(hfl[:, 0:D], hfl[:, D:2 * D], ACT.Square).then_inc(conv_sq, 1)
            sc.wait_ge(group_tr, 1)
            sc.activation(act[0:8, 0, 0:TOK], ps[0:8, 3, P:P + TOK], ACT.Copy).then_inc(group_out, 1)
            hi(U + 10)
            hi(U + 11)
            split_mixed(1, 4, 4, 0, TOK)
            sc.wait_ge(lam_dot, 1)
            sc.activation(st[:, 218:220], st[:, 218:220], ACT.Exp).then_inc(lam_exp, 1)
            for t in range(NT):
                keys = P * (t + 1)
                sc.wait_ge(max_done, t + 1)
                for h in range(HEADS):
                    last_op = sc.activation(L[:, h, 0:keys], L[:, h, 0:keys], ACT.Exp, bias=st[:, 88 + h:89 + h],
                                            accum_out=st[:, 72 + 8 * t + h:73 + 8 * t + h])
                last_op.then_inc(exp_done, 1)
                for g in range(t + 1):
                    if g == 0:
                        sc.wait_ge(p_tr, t + 1)
                        sc.activation(PT[:, 0, :], bank(4, 2), ACT.Copy).then_inc(pt_s, 1)
            for t in range(NT):
                split_mixed(2 + t, 0, 4, t * P, P)
            if last >= 1:
                set_gate(1)
            hi(U + 12)
            hi(U + 13)
            if last >= 1:
                prefetch(1)

            for s in range(1, last + 1):
                split_inputs(s)
                if s in SWIGLUS:
                    swiglu(s)
                    swiglu_end(s)
                elif s == 3:
                    attention()
                else:
                    hgrn()

        @block.vector
        def _(ve):
            link = linked(ve, v_step)

            def lo(unit, lap=0, n=UNIT):
                slot = unit % RING
                ve.wait_ge(w_hi, used(unit, lap))
                ve.tensor_tensor(wlo[:, slot, 0:n], raw[:, slot, 0:n], whi[:, slot, 0:n].bitcast(F32), ALU.subtract)\
                    .then_inc(w_lo, 1)

            def prefetch(s):
                for j in range(2):
                    lo(FIRST[s] + j)

            def ada(group, pieces, kt):
                if not pieces:
                    return
                base, m = piece_base(group[0]), len(group)
                for p in pieces:
                    g, j = divmod(p, 3)
                    s = group[g]
                    ve.wait_ge(acc_bias, 16 * (group[-1] + 1))
                    ve.wait_ge(a_land[j], 16 * ((KT if j == 2 else 0) + KT * (group[0] - 1) + g + 1) + 16 * m * kt)
                    ve.wait_ge(a_used, base + p - 3 * m + 1 + 3 * m * kt)
                    acc = ada_acc[:, s % 2, j * D:(j + 1) * D]
                    ve.scalar_tensor_tensor(acc, ada_raw[:, j, :], csil[:, bass.ds((0 if s < 2 else 8) + kt, 1)], acc,
                                            ALU.mult, ALU.add).then_inc(a_used, 1)

            def set_columns(s):
                par = s % 2
                ve.wait_ge(cols_sum, s + 1)
                link(ve.tensor_copy(modc[:, par, 0:8], ps[:, COL_BANK, 0:8]))
                if s < 2:
                    ve.tensor_scalar(modc[:, par, 8:16], ps[:, COL_BANK, 8:16], 1.0, None, ALU.add).then_inc(cols_set, 1)
                else:
                    g = V_NORM + 8 * (s - 2)
                    ve.scalar_tensor_tensor(modc[:, par, 8:16], ps[:, COL_BANK, 8:16], 1.0, vec[:, g:g + 8],
                                            ALU.add, ALU.mult).then_inc(cols_set, 1)

            def split_inputs(s):
                par = s % 2
                ve.wait_ge(cols_set, s + 1)

                def modulate(n):
                    t, g = divmod(n, 2)
                    ve.wait_ge(h_tr, 4 * s + n + 1)
                    for k in range(4):
                        kt = 4 * g + k
                        done = ve.tensor_scalar(hf[:, kt, t * P:(t + 1) * P], ps[:, n, k * P:(k + 1) * P],
                                                modc[:, par, 8 + kt:9 + kt], modc[:, par, kt:kt + 1], ALU.mult, ALU.add)
                    done.then_inc(h_mod, 1)

                def rest(n):
                    t, g = divmod(n, 2)
                    ve.wait_ge(h_hi, 4 * s + n + 1)
                    part = (slice(None), slice(4 * g, 4 * g + 4), slice(t * P, (t + 1) * P))
                    ve.tensor_tensor(hlo[part], hf[part], hhi[part].bitcast(F32), ALU.subtract).then_inc(h_lo, 1)

                modulate(0)
                for n in range(1, 4):
                    modulate(n)
                    rest(n - 1)
                rest(3)

            def split_mixed(n, k0, k, t0, tn):
                ve.wait_ge(mix_hi, n)
                part = (slice(None), slice(k0, k0 + k), slice(t0, t0 + tn))
                ve.tensor_tensor(hlo[part], hf[part], hhi[part].bitcast(F32), ALU.subtract).then_inc(mix_lo, 1)

            def finish(s):
                ve.wait_ge(gate_set, s + 1)
                for t in range(NT):
                    if t == 0:
                        ve.wait_ge(y_ready, s + 1)
                    else:
                        ve.wait_ge(w_used, used(FIRST[s + 1] - 1))
                    link(ve.tensor_tensor(xn[:, t, :], bank(2 * t, 2), gate[:, s % 2, :], ALU.mult))
                    if s >= 2:
                        ve.tensor_tensor(xs[:, t, :], xs[:, t, :], xn[:, t, :], ALU.add).then_inc(x_new, 1)
                        continue
                    link(ve.scalar_tensor_tensor(xs[:, t, :], xs[:, t, :], ALPHA, xn[:, t, :], ALU.mult, ALU.add))
                    stats = st[:, 12 + 12 * t:24 + 12 * t]
                    for g in range(2):
                        link(ve.bn_stats(stats[:, 6 * g:6 * g + 6], xs[:, t, g * BANK:(g + 1) * BANK]))
                    ve.bn_aggr(st[:, 4 + 2 * t:6 + 2 * t], stats).then_inc(sums_v, 1)
                if s >= 2:
                    return
                ve.wait_ge(ln_land, 32 * (s + 1))
                for t in range(NT):
                    ve.wait_ge(root, LN_ROOT[s] + t + 1)
                    link(ve.tensor_scalar(xs[:, t, :], xs[:, t, :], st[:, 4 + 2 * t:5 + 2 * t], st[:, 5 + 2 * t:6 + 2 * t],
                                          ALU.subtract, ALU.mult))
                    link(ve.tensor_tensor(xs[:, t, :], xs[:, t, :], big[:, 0:D], ALU.mult))
                    ve.tensor_tensor(xs[:, t, :], xs[:, t, :], big[:, D:2 * D], ALU.add).then_inc(x_new, 1)

            def swiglu(s):
                m = SWIGLUS.index(s) * NCH
                U = FIRST[s]
                group = run_ahead.get(s, ())

                def multiply(i):
                    for t in range(NT):
                        ve.wait_ge(silu_done, 2 * (m + i) + t + 1)
                        ve.tensor_tensor(act[:, t, :], act[:, t, :], ps[:, 4 + t, FC:2 * FC], ALU.mult).then_inc(act_ready, 1)

                def alo_of(i):
                    ve.wait_ge(ahi_ready, m + i + 1)
                    ve.tensor_tensor(alo[:, :, :].rearrange("p k n -> p (k n)"), bank(6),
                                     ahi[:, :, :].bitcast(F32).rearrange("p k n -> p (k n)"), ALU.subtract)\
                        .then_inc(alo_ready, 1)

                def body(first, i, lap=0, more=True, kt=None):
                    pieces = list(range(3 * len(group))) if kt is not None else []
                    lo(first + 2, lap)
                    alo_of(i - 1)
                    ada(group, pieces[:3 * len(group) // 2], kt)
                    if more:
                        lo(first + 3, lap)
                    multiply(i)
                    if more:
                        lo(first + 4, lap)
                    ada(group, pieces[3 * len(group) // 2:], kt)

                lo(U + 2)
                multiply(0)
                lo(U + 3)
                body(U + 2, 1)
                with ve.Fori(2, NCH - 1) as i:
                    body(U + 5, i, i - 2, kt=i - 2 if group else None)
                body(U + 3 * (NCH - 1) - 1, NCH - 1, more=False)
                lo(U + UNITS[s] - 1)
                alo_of(NCH - 1)
                if s < last:
                    lo(FIRST[s + 1])
                    set_columns(s + 1)
                    lo(FIRST[s + 1] + 1)
                finish(s)

            ve.wait_ge(vec_tr, 1)
            ve.tensor_copy(vec[:, :], ps[:, 0, 0:NVEC]).then_inc(vec_set, 1)
            ve.wait_ge(csil_set, 1)
            ve.wait_ge(acc_bias, 16)
            for kt in range(KT):
                ve.wait_ge(w_land[kt % RING], 32 * (kt // RING + 1))
                if kt:
                    ve.wait_ge(w_lo, kt)
                ve.scalar_tensor_tensor(ada_acc[:, 0, 0:2 * D], raw[:, kt % RING, :], csil[:, kt:kt + 1],
                                        ada_acc[:, 0, 0:2 * D], ALU.mult, ALU.add).then_inc(w_lo, 1)
            set_columns(0)
            split_inputs(0)
            U = FIRST[0]
            n_b = 4 * (TOKC - BANK)
            lo(U)
            lo(U + 1)
            lo(U + 2, n=n_b)
            ve.wait_ge(lam_land, 16)
            lam = lam_rows.rearrange("p (a b n) -> p a b n", a=2, b=2)
            link(ve.tensor_tensor(lam[:, :, 0, :], lam[:, :, 0, :], lam[:, :, 1, :], ALU.mult))
            ve.tensor_reduce(st[:, 218:220], lam[:, :, 0, :], axis=AX.X, op=ALU.add).then_inc(lam_dot, 1)
            ve.tensor_scalar(st[:, 216:217], vec[:, V_QG:V_QG + 1], 64 ** -0.5, None, ALU.mult).then_inc(gains_set, 1)
            ve.tensor_scalar(st[:, 217:218], vec[:, V_SG:V_SG + 1], 1.0 - LAMBDA_INIT, None, ALU.mult).then_inc(gains_set, 1)
            for kt in range(KT):
                ve.wait_ge(a_land[2], 16 * (kt + 1))
                if kt:
                    ve.wait_ge(a_used, kt)
                acc = ada_acc[:, 0, 2 * D:3 * D]
                ve.scalar_tensor_tensor(acc, ada_raw[:, 2, :], csil[:, kt:kt + 1], acc, ALU.mult, ALU.add).then_inc(a_used, 1)
                if kt == 3:
                    lo(U + 3, n=n_b)
            tok = big[:, 2048:2048 + NT * TOKC].rearrange("p (t n) -> p t n", t=NT)
            L = big[:, 3920:5968].rearrange("p (h k) -> p h k", h=HEADS)
            PT = big[:, 5968:8016].rearrange("p (g n) -> p g n", g=2)
            hfl = hf[:, :, :].rearrange("p k n -> p (k n)")
            xfl = xn[:, :, :].rearrange("p t n -> p (t n)")

            def ada1(kt):
                if 1 in run_ahead.get(0, ()):
                    ada((1,), range(3), kt)

            for t in range(NT):
                if t == 0:
                    ve.wait_ge(blk_ready, 2)
                else:
                    ve.wait_ge(w_used, used(U + 3))
                link(ve.tensor_copy(tok[:, t, BANK:TOKC], ps[:, 6 + t, 0:TOKC - BANK]))
            ve.wait_ge(q_out, 2)
            lo(U + 4)
            lo(U + 5)
            scr = big[:, 8016:8016 + 4 * 144].rearrange("p (m t h n) -> p m t h n", m=4, t=NT, h=9)
            cos = kc[:, C_COS:C_COS + 16].rearrange("p (t n) -> p t n", t=NT).unsqueeze(2).to_broadcast((P, NT, 9, 8))
            sin = kc[:, C_SIN:C_SIN + 16].rearrange("p (t n) -> p t n", t=NT).unsqueeze(2).to_broadcast((P, NT, 9, 8))
            for c0, w in ((0, 64), (QIO, 32)):
                heads = tok[:, :, c0:c0 + 9 * w].rearrange("p t (h n) -> p t h n", h=9)
                x1, x2 = heads[:, :, :, 0:8], heads[:, :, :, 8:16]
                for n, (a, b) in enumerate(((x1, cos), (x2, sin), (x2, cos), (x1, sin))):
                    link(ve.tensor_tensor(scr[:, n], a, b, ALU.mult))
                link(ve.tensor_tensor(x1, scr[:, 0], scr[:, 1], ALU.subtract))
                link(ve.tensor_tensor(x2, scr[:, 2], scr[:, 3], ALU.add))
            kk = big[:, 8592:8848].rearrange("p (t r n) -> p t r n", t=NT, r=2)
            ki4 = big[:, 8848:9104].rearrange("p (t r n) -> p t r n", t=NT, r=4)
            link(ve.tensor_copy(kk, tok[:, :, KO:KO + 64].unsqueeze(2).to_broadcast((P, NT, 2, 64))))
            link(ve.tensor_scalar(tok[:, :, WIO:WIO + 8], tok[:, :, WIO:WIO + 8], IDX_SCALE, None, ALU.mult))
            ve.tensor_copy(ki4, tok[:, :, KIO:KIO + 32].unsqueeze(2).to_broadcast((P, NT, 4, 32))).then_inc(rope_done, 1)
            lo(U + 6)
            ada1(0)
            lo(U + 7)
            ada1(1)
            ve.wait_ge(qk_tr, 2)
            ve.tensor_copy(xfl[:, D:2 * D], bank(6, 2)).then_inc(kT_out, 1)
            lo(U + 8)
            ve.wait_ge(w_used, used(U + 7))
            ve.wait_ge(hc_out, 1)
            u = hf[:, 4:8, :]
            cv = hf[:, 0:4, :]
            ve.tensor_tensor(hfl[:, D:2 * D], hfl[:, 0:D], bank(2, 2), ALU.mult).then_inc(conv_u, 1)
            ve.wait_ge(conv_u, 1)
            lo(U + 9)
            for ct in range(4):
                link(ve.tensor_scalar(cv[:, ct, :], u[:, ct, :], vec[:, V_CW + 8 + ct:V_CW + 9 + ct], None, ALU.mult))
                for j in (1, 2):
                    w = V_CW + 4 * (2 - j) + ct
                    link(ve.scalar_tensor_tensor(cv[:, ct, j:TOK], u[:, ct, 0:TOK - j], vec[:, w:w + 1], cv[:, ct, j:TOK],
                                                 ALU.mult, ALU.add))
            ada1(2)
            ada1(3)
            MARK = -3e38
            kill = big[:, 9104:9360]
            link(ve.tensor_scalar(kill, kc[:, C_CAUSAL:C_CAUSAL + TOK], NEG, None, ALU.add))
            allow = big[:, 9360:9872].rearrange("p (t k) -> p t k", t=NT)
            top8 = st[:, 242:250]
            for t in range(NT):
                keys = P * (t + 1)
                off = TOK - keys
                score = allow[:, t, 0:keys]
                ve.wait_ge(relu_done, t + 1)
                link(ve.scalar_tensor_tensor(score, L[:, 0, 0:keys], tok[:, t, WIO:WIO + 1],
                                             kc[:, C_CAUSAL + off:C_CAUSAL + TOK], ALU.mult, ALU.add))
                for h in range(1, HEADS):
                    step = ve.scalar_tensor_tensor(score, L[:, h, 0:keys], tok[:, t, WIO + h:WIO + h + 1], score,
                                                   ALU.mult, ALU.add)
                    if h < HEADS - 1:
                        link(step)
                step.then_inc(score_done, 1)
                ve.wait_ge(score_done, t + 1)
                for n in range(TOPK // 8):
                    link(ve.max(top8, score))
                    link(ve.match_replace(score, top8, score, MARK))
                link(ve.tensor_scalar(score, score, MARK, -NEG, ALU.is_equal, ALU.mult))
                link(ve.tensor_tensor(score, score, kill[:, off:TOK], ALU.add))
                if t == 0:
                    ve.wait_ge(w_used, used(U + 9))
                    ve.tensor_tensor(hfl[:, D:2 * D], hfl[:, 0:D], bank(0, 2), ALU.mult).then_inc(conv_gated, 1)
                    for kt in range(4, 8):
                        ada1(kt)
            ve.wait_ge(group_mm, 1)
            ve.tensor_copy(st[:, 40:56], ps[:, 3, 0:16]).then_inc(sums_v, 1)
            lo(U + 10)
            lo(U + 11)

            def logits(t):
                keys = P * (t + 1)
                ve.wait_ge(att_mm, t + 1)
                if t:
                    ve.wait_ge(p_tr, t)
                mask = allow[:, t, 0:keys].unsqueeze(1).to_broadcast((P, 4, keys))
                for r in range(2):
                    ins = bank(4 + 2 * r, 2).rearrange("p (j k) -> p j k", j=4)[:, :, 0:keys]
                    link(ve.scalar_tensor_tensor(L[:, 4 * r:4 * r + 4, 0:keys], ins, 0.125, mask, ALU.mult, ALU.add))
                ve.tensor_reduce(st[:, 88:96], L[:, :, 0:keys], axis=AX.X, op=ALU.max, negate=True).then_inc(max_done, 1)

            def heads_out(t):
                O = ps[:, 2 + t, :]
                ob = big[:, 3920 + BANK * t:3920 + BANK * (t + 1)]
                sq = big[:, 3920 + BANK * (2 + t):3920 + BANK * (3 + t)]
                link(ve.reciprocal(st[:, 104 + 8 * t:112 + 8 * t], st[:, 72 + 8 * t:80 + 8 * t]))
                ve.wait_ge(pv_mm, t + 1)
                link(ve.tensor_tensor(ob.rearrange("p (j r d) -> p r j d", j=4, r=2), O.rearrange("p (r j d) -> p r j d", r=2, j=4),
                                      st[:, 104 + 8 * t:112 + 8 * t].rearrange("p (r j) -> p r j", r=2).unsqueeze(3)
                                      .to_broadcast((P, 2, 4, 64)), ALU.mult))
                link(ve.tensor_tensor(sq, ob, ob, ALU.mult))
                ve.tensor_reduce(st[:, 120 + 8 * t:128 + 8 * t], sq.rearrange("p (h d) -> p h d", h=HEADS), axis=AX.X, op=ALU.add)\
                    .then_inc(sums_v, 1)

            def heads_norm(t):
                ob = big[:, 3920 + BANK * t:3920 + BANK * (t + 1)].rearrange("p (h d) -> p h d", h=HEADS)
                ve.wait_ge(root, ATT_ROOT[0] + t + 1)
                ve.tensor_tensor(ob, ob, st[:, 120 + 8 * t:128 + 8 * t].unsqueeze(2).to_broadcast((P, HEADS, 64)), ALU.mult)\
                    .then_inc(o_done, 1)

            def pt_evac(t):
                if t:
                    ve.wait_ge(p_tr, t + 1)
                    ve.tensor_copy(PT[:, 1, :], bank(6, 2)).then_inc(pt_v, 1)

            logits(0)
            ve.wait_ge(spread_mm, 1)
            link(ve.tensor_tensor(hfl[:, D:2 * D], hfl[:, D:2 * D], bank(0, 2), ALU.mult))
            ve.tensor_tensor(hf[:, 4:8, :], hf[:, 4:8, :], vec[:, V_CG:V_CG + 4].unsqueeze(2).to_broadcast((P, 4, TOK)), ALU.mult)\
                .then_inc(mix_f, 1)
            split_mixed(1, 4, 4, 0, TOK)
            logits(1)
            pt_evac(1)
            heads_out(0)
            heads_out(1)
            for t in range(NT):
                heads_norm(t)
            for t in range(NT):
                ve.wait_ge(o_tr, t + 1)
                ve.tensor_tensor(hf[:, 0:4, t * P:(t + 1) * P], ps[:, 4 + t, :].rearrange("p (k n) -> p k n", k=4),
                                 vec[:, V_AG:V_AG + 4].unsqueeze(2).to_broadcast((P, 4, P)), ALU.mult).then_inc(mix_f, 1)
                split_mixed(2 + t, 0, 4, t * P, P)
            ve.wait_ge(lam_exp, 1)
            link(ve.tensor_tensor(st[:, 220:221], st[:, 219:220], st[:, 218:219], ALU.subtract))
            link(ve.tensor_scalar(st[:, 221:222], st[:, 220:221], -LAMBDA_INIT, None, ALU.add))
            if last >= 1:
                set_columns(1)
            lo(U + 12)
            lo(U + 13)
            if last >= 1:
                prefetch(1)
            finish(0)

            def attention():
                U = FIRST[3]
                with ve.Fori(0, 2) as i:
                    lo(U + 2, 2 * i)
                    lo(U + 3, 2 * i)
                    for b in range(2):
                        for t in range(NT):
                            n = 2 * b + t
                            ve.wait_ge(qk_sq, 4 * i + n + 1)
                            ve.tensor_reduce(st[:, 152 + 8 * n:160 + 8 * n],
                                             big[:, 8192 + n * BANK:8192 + (n + 1) * BANK].rearrange("p (h d) -> p h d", h=8),
                                             axis=AX.X, op=ALU.add).then_inc(sums_v, 1)
                        lo(U + 4 + 2 * b, 2 * i)
                        for t in range(NT):
                            n = 2 * b + t
                            ve.wait_ge(root, QK_ROOT + 4 * i + n + 1)
                            ve.tensor_tensor(qkv[:, t, bass.ds(b * D + i * BANK, BANK)].rearrange("p (h d) -> p h d", h=8),
                                             bank(n).rearrange("p (h d) -> p h d", h=8),
                                             st[:, 152 + 8 * n:160 + 8 * n].unsqueeze(2).to_broadcast((P, 8, 64)), ALU.mult)\
                                .then_inc(qk_out, 1)
                        lo(U + 5 + 2 * b, 2 * i)
                for t in range(NT):
                    for g in range(2):
                        ve.wait_ge(qk_tr, 2 + 4 * t + 2 * g + 2)
                        ve.tensor_scalar(kT[:, 4 * g:4 * g + 4, t * P:(t + 1) * P],
                                         bank(4 * t + 2 * g + 1).rearrange("p (h n) -> p h n", h=4),
                                         vec[:, V_KG:V_KG + 1], None, ALU.mult).then_inc(kT3, 1)

                def add_bias(i):
                    t, h = divmod(i, HEADS)
                    keys = P * (t + 1)
                    ve.wait_ge(dot_mm, i + 1)
                    if t == 0 and i == 0:
                        ve.wait_ge(toe_land, 64)
                    s_ = soft[:, i % 2, :, 0:keys]
                    link(ve.tensor_tensor(s_, bank(2 * (i % 2), 2).rearrange("p (c k) -> p c k", c=2)[:, :, 0:keys],
                                          relb[:, h, TOK - keys:TOK].unsqueeze(1).to_broadcast((P, 2, keys)), ALU.add))
                    ve.tensor_reduce(st[:, 88 + 2 * (i % 2):90 + 2 * (i % 2)], s_, axis=AX.X, op=ALU.max, negate=True)\
                        .then_inc(sm_ready, 1)

                def combine(i):
                    keys = P * (i // HEADS + 1)
                    r = st[:, 104 + 2 * (i % 2):106 + 2 * (i % 2)]
                    ve.wait_ge(sm_exp, i + 1)
                    link(ve.reciprocal(r, st[:, 72 + 2 * (i % 2):74 + 2 * (i % 2)]))
                    link(ve.tensor_scalar(soft[:, i % 2, 1, 0:keys], soft[:, i % 2, 1, 0:keys], r[:, 1:2], st[:, 221:222],
                                          ALU.mult, ALU.mult))
                    ve.scalar_tensor_tensor(soft[:, i % 2, 0, 0:keys], soft[:, i % 2, 0, 0:keys], r[:, 0:1],
                                            soft[:, i % 2, 1, 0:keys], ALU.mult, ALU.add).then_inc(a_ready, 1)

                def sum_heads(t):
                    ve.wait_ge(head_sq, t + 1)
                    ve.tensor_reduce(st[:, 120 + 8 * t:128 + 8 * t], qkv[:, t, D:2 * D].rearrange("p (h d) -> p h d", h=HEADS),
                                     axis=AX.X, op=ALU.add).then_inc(sums_v, 1)

                def norm_heads(t):
                    ve.wait_ge(root, ATT_ROOT[3] + t + 1)
                    ve.tensor_tensor(qkv[:, t, 0:D].rearrange("p (h d) -> p h d", h=HEADS),
                                     bank(6, 2).rearrange("p (h d) -> p h d", h=HEADS),
                                     st[:, 120 + 8 * t:128 + 8 * t].unsqueeze(2).to_broadcast((P, HEADS, P)), ALU.mult)\
                        .then_inc(o_done, 1)

                for i in range(2 * HEADS):
                    if i >= 2:
                        ve.wait_ge(a_tr, i - 1)
                    add_bias(i)
                    if i:
                        combine(i - 1)
                    if i == HEADS + 2:
                        sum_heads(0)
                        norm_heads(0)
                combine(2 * HEADS - 1)
                sum_heads(1)
                norm_heads(1)
                for t in range(NT):
                    for g in range(2):
                        n = 2 * t + g
                        ve.wait_ge(o_tr, 2 + n + 1)
                        ve.tensor_scalar(hf[:, 4 * g:4 * g + 4, t * P:(t + 1) * P], bank(n).rearrange("p (k n) -> p k n", k=4),
                                         st[:, 217:218], None, ALU.mult).then_inc(mix_f, 1)
                        if n:
                            g1, t1 = (n - 1) % 2, (n - 1) // 2
                            split_mixed(3 + n, 4 * g1, 4, t1 * P, P)
                split_mixed(7, 4, 4, P, P)
                if last > 3:
                    set_columns(4)
                lo(U + 14)
                lo(U + 15)
                if last > 3:
                    lo(FIRST[4])
                    lo(FIRST[4] + 1)
                finish(3)

            def hgrn():
                U = FIRST[6]
                ve.tensor_tensor(lb, vec[:, V_LB:V_LB + 8], vec[:, V_LB:V_LB + 8], ALU.subtract).then_inc(lb_diff, 1)
                lo(U + 2)
                lo(U + 3)

                def forget(b):
                    heads = slice(4 * b, 4 * b + 4)
                    G, k, e1 = h_G[:, heads, :], h_k[:, heads, :], hf[:, heads, :]
                    f = bank(2 * b, 2).rearrange("p (h n) -> p h n", h=4)
                    e0 = xn[:, b, :].rearrange("p (h n) -> p h n", h=4)
                    lo(U + 4 + 3 * b)
                    ve.wait_ge(f_log, b + 1)
                    link(ve.scalar_tensor_tensor(G, f, 0.0, e0, ALU.min, ALU.subtract))
                    ve.tensor_tensor(k, G, f, ALU.subtract)
                    ve.tensor_scalar(e1, f, -80.0, None, ALU.max).then_inc(f_taken, 1)
                    lo(U + 5 + 3 * b)
                    if b == 0:
                        ve.wait_ge(lb_exp, 1)
                        link(ve.reciprocal(one_less_lb, lb))
                        link(ve.tensor_tensor(one_less_lb, lb, one_less_lb, ALU.mult))
                        link(ve.tensor_tensor(lb, one_less_lb, one_less_lb, ALU.subtract))
                        ve.tensor_scalar(one_less_lb, lb, -1.0, 1.0, ALU.mult, ALU.add).then_inc(lb_diff, 1)
                        ve.wait_ge(lb_diff, 2)
                    ve.wait_ge(f_exp, b + 1)
                    link(ve.tensor_tensor(G, G, e1, ALU.add))
                    ve.tensor_tensor(k, k, one_less_lb[:, heads].unsqueeze(2).to_broadcast((P, 4, TOK)), ALU.mult)
                    ve.wait_ge(scan_set, 3)
                    for h in range(0, 4, 2):
                        part = h_G[:, 4 * b + h:4 * b + h + 2, :].rearrange("p h n -> p (h n)")
                        done = ve.tensor_tensor_scan(part, chunk_carry, part, 0.0, ALU.mult, ALU.add)
                    done.then_inc(k_ready, 1)

                def differences(level):
                    E = decayed(level)
                    if level >= 3:
                        ve.wait_ge(lv_mm, 2 * (level - 1))
                    if level == 1:
                        ve.wait_ge(k_ready, 2)
                    if level <= len(LEVELS):
                        n = LEVELS[level - 1]
                        e, g = halves(E, level), halves(h_G, level)
                        middle = g[:, :, 0, n - 1:n].to_broadcast((P, HEADS * TOK // (2 * n), n))
                        done = ve.tensor_tensor(e[:, :, 0, :], middle, g[:, :, 0, :], ALU.subtract)
                        if level > 1:
                            done = ve.tensor_tensor(e[:, :, 1, :], g[:, :, 1, :], middle, ALU.subtract)
                    else:
                        e, g = (a.rearrange("p h (c n) -> p h c n", n=CHUNK) for a in (E, h_G))
                        total = [g[:, :, c, CHUNK - 1:CHUNK].to_broadcast((P, HEADS, CHUNK)) for c in range(3)]
                        link(ve.tensor_tensor(e[:, :, 0, :], total[0], g[:, :, 0, :], ALU.subtract))
                        ve.tensor_tensor(e[:, :, 0, :], e[:, :, 0, :], total[1], ALU.add)
                        ve.tensor_tensor(e[:, :, 1, :], total[1], g[:, :, 1, :], ALU.subtract)
                        done = ve.tensor_tensor(e[:, :, 3, :], g[:, :, 3, :], total[2], ALU.add)
                    done.then_inc(lv_sub, 1)

                def decay(level):
                    e, k, q = (halves(a, level) for a in (decayed(level), h_k, h_q))
                    ve.wait_ge(lv_exp, level)
                    ve.tensor_tensor(e[:, :, 0, :], e[:, :, 0, :], k[:, :, 0, :], ALU.mult)
                    if level == 1:
                        ve.wait_ge(q_copied, 2)
                    ve.tensor_tensor(e[:, :, 1, :], e[:, :, 1, :], q[:, :, 1, :], ALU.mult).then_inc(lv_mul, 1)

                def take_scores(level):
                    if level == 0:
                        ve.wait_ge(mask_land, 16)
                    for t in range(NT if level <= len(LEVELS) else 1):
                        ve.wait_ge(lv_mm, 2 * level + t + 1)
                        products = by_head(bank(4 + 2 * t, 2))
                        if level <= len(LEVELS):
                            if level:
                                ve.wait_ge(lv_copy, 2 * level - 1 + t)
                            done = ve.copy_predicated(scoresT[:, HEADS * t:HEADS * (t + 1), :],
                                                      mask8[:, level, :].unsqueeze(1).to_broadcast((P, HEADS, P)), products)
                        else:
                            done = ve.tensor_copy(scoresT[:, 2 * HEADS:3 * HEADS, :], products)
                        done.then_inc(lv_copy, 1)

                forget(0)
                lo(U + 6)
                forget(1)
                differences(1)
                lo(U + 9)
                lo(U + 10)
                for level in range(len(LEVELS) + 2):
                    if level:
                        decay(level)
                        take_scores(level - 1)
                        if level <= len(LEVELS):
                            differences(level + 1)
                    if level <= 7:
                        lo(U + 11 + level)
                take_scores(len(LEVELS) + 1)
                for t in range(NT):
                    ve.wait_ge(head_sq, 2 + t + 1)
                    ve.tensor_reduce(st[:, 120 + 8 * t:128 + 8 * t], xn[:, t, :].rearrange("p (h d) -> p h d", h=HEADS),
                                     axis=AX.X, op=ALU.add).then_inc(sums_v, 1)
                ve.wait_ge(g_silu, 1)
                for t in range(NT):
                    ve.wait_ge(root, ATT_ROOT[6] + t + 1)
                    o = h_o[:, t, :].rearrange("p (h d) -> p h d", h=HEADS)
                    link(ve.tensor_tensor(o, bank(2 * t, 2).rearrange("p (h d) -> p h d", h=HEADS),
                                          st[:, 120 + 8 * t:128 + 8 * t].unsqueeze(2).to_broadcast((P, HEADS, P)), ALU.mult))
                    ve.tensor_tensor(h_o[:, t, :], h_o[:, t, :], h_g[:, t, :], ALU.mult).then_inc(o_done, 1)
                for n in range(2 * NT + 1):
                    t, g = divmod(n, 2)
                    if n < 2 * NT:
                        ve.wait_ge(o_tr, 6 + n + 1)
                        ve.tensor_tensor(hf[:, 4 * g:4 * g + 4, t * P:(t + 1) * P], bank(n).rearrange("p (k n) -> p k n", k=4),
                                         vec[:, V_OG + 4 * g:V_OG + 4 * g + 4].unsqueeze(2).to_broadcast((P, 4, P)), ALU.mult)\
                            .then_inc(mix_f, 1)
                    if n:
                        split_mixed(7 + n, 4 * ((n - 1) % 2), 4, (n - 1) // 2 * P, P)
                if last > 6:
                    set_columns(7)
                lo(U + 19)
                if last > 6:
                    lo(FIRST[7])
                    lo(FIRST[7] + 1)
                finish(6)

            for s in range(1, last + 1):
                split_inputs(s)
                if s in SWIGLUS:
                    swiglu(s)
                elif s == 3:
                    attention()
                else:
                    hgrn()

        @block.tensor
        def _(pe):
            def three(dst, xh, xl, wh, wl, first, final, weights_move=True):
                for n, (a, w) in enumerate(((xh, wh), (xh, wl), (xl, wh))):
                    lhsT, rhs = (a, w) if weights_move else (w, a)
                    done = pe.matmul(dst, lhsT, rhs, start=first and n == 0, stop=final and n == 2, skip_group_check=True)
                return done

            def columns_by_token(unit, g, banks, n=BANK, lap=0, ready=None):
                slot = unit % RING
                pe.wait_ge(w_lo, unit + 1 + RING * lap)
                for t in range(NT):
                    for k in range(4):
                        kt = 4 * g + k
                        tok_cols = slice(t * P, (t + 1) * P)
                        done = three(ps[:, banks[t], 0:n], hhi[:, kt, tok_cols], hlo[:, kt, tok_cols],
                                     whi[:, slot, k * n:(k + 1) * n], wlo[:, slot, k * n:(k + 1) * n],
                                     g == 0 and k == 0, g == 1 and k == 3)
                    if g == 1 and t == 0:
                        done.then_inc(ready, 1)
                done.then_inc(w_used, 1)

            def columns_by_feature(unit, g, b):
                slot = unit % RING
                pe.wait_ge(w_lo, unit + 1)
                for ct in range(4):
                    dst = psf[:, b * BANK + ct * TOK:b * BANK + (ct + 1) * TOK]
                    for k in range(4):
                        kt, cols = 4 * g + k, slice(k * BANK + ct * P, k * BANK + (ct + 1) * P)
                        done = three(dst, hhi[:, kt, :], hlo[:, kt, :], whi[:, slot, cols], wlo[:, slot, cols],
                                     g == 0 and k == 0 and ct % 2 == 0, g == 1 and k == 3, weights_move=False)
                done.then_inc(w_used, 1)

            def down_rows(unit, hi_of, lo_of, first, final, lap=0, before=None, end=None):
                slot = unit % RING
                pe.wait_ge(w_lo, unit + 1 + RING * lap)
                for t in range(NT):
                    if before:
                        before(t)
                    for h in range(2):
                        for k in range(2):
                            cols = slice(k * D + h * BANK, k * D + (h + 1) * BANK)
                            done = three(bank(2 * t + h), hi_of(k, t), lo_of(k, t), whi[:, slot, cols], wlo[:, slot, cols],
                                         first and k == 0, final and k == 1)
                    if final and t == 0:
                        done.then_inc(y_ready, 1)
                done.then_inc(w_used, 1)

            def transposes(blocks, b, signal):
                for n, a in enumerate(blocks):
                    done = pe.transpose(ps[:, b, n * P:(n + 1) * P], a, ident)
                done.then_inc(signal, 1)

            def sum_columns(s):
                if s == 0:
                    pe.wait_ge(w_lo, KT)
                else:
                    pe.wait_ge(a_used, piece_base(max(g for v in run_ahead.values() for g in v if s in v)) + 3 * KT)
                    pe.wait_ge(cols_set, s)
                for j in range(16):
                    done = pe.matmul(ps[:, COL_BANK, j:j + 1], ada_acc[:, s % 2, j * P:(j + 1) * P], ones[:, 0:1],
                                     start=True, stop=True)
                done.then_inc(cols_sum, 1)

            def sum_gate(s):
                if s == 0:
                    pe.wait_ge(a_used, KT)
                for h in range(2):
                    done = pe.matmul(bank(GATE_BANK(s) + h), ones[:, :], ada_acc[:, s % 2, 2 * D + h * BANK:2 * D + (h + 1) * BANK],
                                     start=True, stop=True)
                done.then_inc(gate_sum, 1)

            def transpose_inputs(s):
                for t in range(NT):
                    if s == 0:
                        pe.wait_ge(x_land, 32)
                        pe.wait_ge(vec_set, 1)
                    elif s == 1:
                        pe.wait_ge(x_new, t + 1)
                    else:
                        pe.wait_ge(h_src, 2 * (s - 2) + t + 1)
                    src = xs if s < 2 else xn
                    for g in range(2):
                        transposes([src[:, t, (4 * g + k) * P:(4 * g + k + 1) * P] for k in range(4)], 2 * t + g, h_tr)

            def output_product(s, unit, mix_first):
                if s < last:
                    sum_columns(s + 1)
                    sum_gate(s + 1)
                for j in range(4):
                    def before(t):
                        if j == 0:
                            pe.wait_ge(mix_lo, mix_first[t])
                    down_rows(unit + j, lambda k, t: hhi[:, 2 * j + k, t * P:(t + 1) * P],
                              lambda k, t: hlo[:, 2 * j + k, t * P:(t + 1) * P], j == 0, j == 3, before=before)

            def swiglu(s):
                m = SWIGLUS.index(s) * NCH
                U = FIRST[s]

                def gate_up(unit, g, i, lap=0, first_chunk=False):
                    if g == 0 and not first_chunk:
                        pe.wait_ge(act_ready, 2 * (m + i))
                    if first_chunk:
                        pe.wait_ge(h_lo, 4 * s + 3 + g)
                    columns_by_token(unit, g, (4, 5), lap=lap, ready=gu_ready)

                def turn(i):
                    pe.wait_ge(act_ready, 2 * (m + i + 1))
                    pe.wait_ge(alo_ready, m + i)
                    for k in range(2):
                        for t in range(NT):
                            done = pe.transpose(ps[:, 6, k * TOK + t * P:k * TOK + (t + 1) * P],
                                                act[:, t, k * P:(k + 1) * P], ident)
                    done.then_inc(tr_ready, 1)

                def down(unit, i, lap=0, first=False, final=False):
                    pe.wait_ge(alo_ready, m + i + 1)
                    down_rows(unit, lambda k, t: ahi[:, k, t * P:(t + 1) * P], lambda k, t: alo[:, k, t * P:(t + 1) * P],
                              first, final, lap=lap)

                def body(first, i, lap=0, first_down=False):
                    gate_up(first, 0, i, lap)
                    turn(i - 1)
                    gate_up(first + 1, 1, i, lap)
                    down(first + 2, i - 1, lap, first=first_down)

                gate_up(U, 0, 0, first_chunk=True)
                gate_up(U + 1, 1, 0, first_chunk=True)
                body(U + 2, 1, first_down=True)
                if s == 1 and last >= 3:
                    pe.wait_ge(toe_fill, 2)
                    pe.wait_ge(cols_set, 2)
                    for h in range(HEADS):
                        if h >= 2:
                            pe.wait_ge(toe_rows, h - 1)
                        pe.matmul(ps[:, 6 + h % 2, 0:TOE], big[0:BUCKETS + 1, 2560 + h * P:2560 + (h + 1) * P],
                                  big[0:BUCKETS + 1, 2048:2048 + TOE], start=True, stop=True).then_inc(toe_mm, 1)
                    pe.wait_ge(toe_rows, HEADS)
                with pe.Fori(2, NCH - 1) as i:
                    body(U + 5, i, i - 2)
                body(U + 3 * (NCH - 1) - 1, NCH - 1)
                turn(NCH - 1)
                if s < last:
                    sum_columns(s + 1)
                    sum_gate(s + 1)
                down(U + UNITS[s] - 1, NCH - 1, final=True)

            def attention():
                U = FIRST[3]
                pe.wait_ge(h_lo, 16)
                with pe.Fori(0, 2) as i:
                    for b in range(3):
                        for g in range(2):
                            columns_by_token(U + 2 * b + g, g, (2 * b, 2 * b + 1), lap=2 * i, ready=blk_ready)
                    pe.wait_ge(qk_out, 4 * i + 4)
                    pe.wait_ge(v_out, 2 * i + 2)
                for t in range(NT):
                    for g in range(2):
                        for b in range(2):
                            transposes([qkv[:, t, b * D + (4 * g + h) * P:b * D + (4 * g + h + 1) * P] for h in range(4)],
                                       4 * t + 2 * g + b, qk_tr)

                def dots(i):
                    t, h = divmod(i, HEADS)
                    keys = P * (t + 1)
                    if i == 0:
                        pe.wait_ge(qT3, 4)
                        pe.wait_ge(kT3, 4)
                    if i >= 2:
                        pe.wait_ge(sm_ready, i - 1)
                    for c in range(2):
                        rows = slice(64 * c, 64 * c + 64)
                        done = pe.matmul(ps[:, 2 * (i % 2) + c, 0:keys], qT[rows, h, t * P:(t + 1) * P], kT[rows, h, 0:keys],
                                         start=True, stop=True)
                    done.then_inc(dot_mm, 1)

                def turn(i):
                    pe.wait_ge(a_ready, i + 1)
                    if i >= 2:
                        pe.wait_ge(aT_out, i - 1)
                    for g in range(i // HEADS + 1):
                        done = pe.transpose(ps[:, 4 + i % 2, g * P:(g + 1) * P], soft[:, i % 2, 0, g * P:(g + 1) * P], ident)
                    done.then_inc(a_tr, 1)

                def values(i):
                    t, h = divmod(i, HEADS)
                    pe.wait_ge(aT_out, i + 1)
                    if i == HEADS:
                        pe.wait_ge(o_done, 2 + 1)
                    for g in range(t + 1):
                        done = pe.matmul(psf[:, 6 * BANK + h * P:6 * BANK + (h + 1) * P], weightsT[:, i % 2, g * P:(g + 1) * P],
                                         qkv[:, g, 2 * D + h * P:2 * D + (h + 1) * P], start=g == 0, stop=g == t)
                    done.then_inc(av_mm, 1)

                for i in range(2 * HEADS):
                    dots(i)
                    if i:
                        turn(i - 1)
                    if i >= 2:
                        values(i - 2)
                turn(2 * HEADS - 1)
                values(2 * HEADS - 2)
                values(2 * HEADS - 1)
                for t in range(NT):
                    pe.wait_ge(o_done, 2 + t + 1)
                    for g in range(2):
                        transposes([qkv[:, t, (4 * g + k) * P:(4 * g + k + 1) * P] for k in range(4)], 2 * t + g, o_tr)
                output_product(3, U + 12, (5, 7))

            def hgrn():
                U = FIRST[6]
                for g in range(2):
                    if g == 0:
                        pe.wait_ge(h_lo, 28)
                    columns_by_feature(U + g, g, 0)
                for g in range(2):
                    columns_by_feature(U + 2 + g, g, 2)
                for b in range(2):
                    pe.wait_ge(f_taken, b + 1)
                    for g in range(2):
                        columns_by_feature(U + 4 + 2 * b + g, g, 2 * b)

                def scores(level):
                    for t in range(NT if level <= len(LEVELS) else 1):
                        if level:
                            pe.wait_ge(lv_copy, 2 * level - 1 + t)
                        cols = slice(t * P, (t + 1) * P)
                        for h in range(HEADS):
                            dst = psf[:, (4 + 2 * t) * BANK + h * P:(4 + 2 * t) * BANK + (h + 1) * P]
                            if level == 0:
                                lhsT, rhs = h_k[:, h, cols], h_q[:, h, cols]
                            elif level <= len(LEVELS):
                                lhsT = rhs = decayed(level)[:, h, cols]
                            else:
                                lhsT, rhs = decayed(level)[:, h, 0:P], decayed(level)[:, h, P:TOK]
                            done = pe.matmul(dst, lhsT, rhs, start=True, stop=True)
                        done.then_inc(lv_mm, 1)

                for level in range(len(LEVELS) + 2):
                    if level <= 7:
                        b, g = divmod(level, 2)
                        if g == 0:
                            if b < 2:
                                pe.wait_ge(q_copied, b + 1)
                            else:
                                pe.wait_ge(vg_out, 2 * (b - 1))
                        columns_by_token(U + 8 + level, g, (2 * (b % 2), 2 * (b % 2) + 1), ready=blk_ready)
                    if level == 0:
                        pe.wait_ge(k_ready, 2)
                        pe.wait_ge(q_copied, 2)
                    else:
                        pe.wait_ge(lv_mul, level)
                    scores(level)
                pe.wait_ge(lv_copy, 2 * (len(LEVELS) + 1) + 1)
                pe.wait_ge(vg_out, 8)
                for t in range(NT):
                    for h in range(HEADS):
                        cols = slice(h * P, (h + 1) * P)
                        dst = psf[:, 2 * t * BANK + h * P:2 * t * BANK + (h + 1) * P]
                        done = pe.matmul(dst, scoresT[:, HEADS * t + h, :], h_v[:, t, cols], start=True, stop=t == 0)
                        if t:
                            done = pe.matmul(dst, scoresT[:, 2 * HEADS + h, :], h_v[:, 0, cols], start=False, stop=True)
                    done.then_inc(pv_mm, 1)
                for t in range(NT):
                    pe.wait_ge(o_done, 4 + t + 1)
                    for g in range(2):
                        transposes([h_o[:, t, (4 * g + k) * P:(4 * g + k + 1) * P] for k in range(4)], 2 * t + g, o_tr)
                output_product(6, U + 16, (9, 11))

            pe.wait_ge(const_land, 16)
            pe.wait_ge(vec_land, 208)
            pe.transpose(ps[:, 0, 0:NVEC], big[0:NVEC, 0:P], kc[0:NVEC, C_ID:C_ID + NVEC]).then_inc(vec_tr, 1)
            pe.wait_ge(ones_set, 3)
            sum_columns(0)
            transpose_inputs(0)
            U = FIRST[0]
            tok = big[:, 2048:2048 + NT * TOKC].rearrange("p (t n) -> p t n", t=NT)
            L = big[:, 3920:5968].rearrange("p (h k) -> p h k", h=HEADS)
            PT = big[:, 5968:8016].rearrange("p (g n) -> p g n", g=2)
            xfl = xn[:, :, :].rearrange("p t n -> p (t n)")
            kk = big[:, 8592:8848].rearrange("p (t n) -> p t n", t=NT)
            ki4 = big[:, 8848:9104].rearrange("p (t n) -> p t n", t=NT)
            pe.wait_ge(h_lo, 4)
            pe.wait_ge(cols_set, 1)
            for g in range(2):
                columns_by_token(U + g, g, (4, 5), ready=blk_ready)
            for g in range(2):
                columns_by_token(U + 2 + g, g, (6, 7), n=TOKC - BANK, ready=blk_ready)
            for g in range(2):
                columns_by_feature(U + 4 + g, g, 0)
            pe.wait_ge(rope_done, 1)
            pe.wait_ge(q_out, 2)
            sources = [lambda t, j=j: tok[:, t, j * P:(j + 1) * P] for j in range(4)]
            sources += [lambda t: kk[:, t, :]] + [lambda t, j=j: tok[:, t, QIO + j * P:QIO + (j + 1) * P] for j in range(2)]
            sources += [lambda t: ki4[:, t, :]]
            for n, src in enumerate(sources):
                for t in range(NT):
                    done = pe.transpose(psf[:, 4 * BANK + n * TOK + t * P:4 * BANK + n * TOK + (t + 1) * P], src(t), ident)
                if n in (3, 7):
                    done.then_inc(qk_tr, 1)
            for g in range(2):
                columns_by_feature(U + 6 + g, g, 2)

            def index_products(t):
                keys = P * (t + 1)
                for j in range(2):
                    for r in range(4):
                        rows = slice(32 * r, 32 * r + 32)
                        done = pe.matmul(ps[:, 4 + r, j * keys:(j + 1) * keys],
                                         xfl[rows, D + TOK * (1 + j) + t * P:D + TOK * (1 + j) + (t + 1) * P],
                                         xfl[rows, D + 3 * TOK:D + 3 * TOK + keys], start=True, stop=True)
                done.then_inc(idx_mm, 1)

            pe.wait_ge(qT_out, 1)
            pe.wait_ge(kT_out, 1)
            index_products(0)
            pe.wait_ge(hc_out, 1)
            for g in range(2):
                columns_by_feature(U + 8 + g, g, 0)
            pe.wait_ge(relu_done, 1)
            index_products(1)
            pe.wait_ge(conv_u, 1)
            sum_gate(0)

            def logit_products(t):
                keys = P * (t + 1)
                for j in range(4):
                    for r in range(2):
                        rows = slice(64 * r, 64 * r + 64)
                        at_col = (4 + 2 * r) * BANK + j * TOK
                        done = pe.matmul(psf[:, at_col:at_col + keys], xfl[rows, j * TOK + t * P:j * TOK + (t + 1) * P],
                                         xfl[rows, D:D + keys], start=True, stop=True)
                done.then_inc(att_mm, 1)

            def attend(t):
                pe.wait_ge(exp_done, t + 1)
                for g in range(t + 1):
                    for h in range(HEADS):
                        done = pe.transpose(psf[:, (4 + 2 * g) * BANK + h * P:(4 + 2 * g) * BANK + (h + 1) * P],
                                            L[:, h, g * P:(g + 1) * P], ident)
                done.then_inc(p_tr, 1)
                pe.wait_ge(pt_s, t + 1)
                if t:
                    pe.wait_ge(pt_v, 1)
                for h in range(HEADS):
                    for g in range(t + 1):
                        done = pe.matmul(ps[:, 2 + t, h * 64:(h + 1) * 64], PT[:, g, h * P:(h + 1) * P],
                                         tok[:, g, VO:VO + 64], start=g == 0, stop=g == t)
                done.then_inc(pv_mm, 1)

            pe.wait_ge(conv_sq, 1)
            pe.wait_ge(gate_set, 1)
            for t in range(NT):
                for ct in range(4):
                    done = pe.matmul(ps[:, 3, 8 * t + 2 * ct:8 * t + 2 * ct + 2], hf[:, ct, t * P:(t + 1) * P],
                                     kc[:, C_HALF:C_HALF + 2], start=True, stop=True)
            done.then_inc(group_mm, 1)
            pe.wait_ge(score_done, 2)
            logit_products(0)
            pe.wait_ge(root, 1)
            for t in range(NT):
                done = pe.transpose(ps[0:8, 3, P + t * P:P + (t + 1) * P], st[:, 40 + 8 * t:48 + 8 * t], ident)
            done.then_inc(group_tr, 1)
            pe.wait_ge(group_out, 1)
            pe.wait_ge(spread_land, 16)
            for ct in range(4):
                done = pe.matmul(psf[:, ct * TOK:(ct + 1) * TOK], gate[0:8, 1, ct * P:(ct + 1) * P], act[0:8, 0, 0:TOK],
                                 start=True, stop=True)
            done.then_inc(spread_mm, 1)
            attend(0)
            logit_products(1)
            attend(1)
            for t in range(NT):
                pe.wait_ge(o_done, t + 1)
                transposes([big[:, 3920 + BANK * t + j * P:3920 + BANK * t + (j + 1) * P] for j in range(4)], 4 + t, o_tr)
            pe.wait_ge(mix_f, 3)
            output_product(0, U + 10, (3, 3))

            for s in range(1, last + 1):
                transpose_inputs(s)
                if s in SWIGLUS:
                    swiglu(s)
                elif s == 3:
                    attention()
                else:
                    hgrn()


INPUTS = (
    "x c w_ada b_ada w_in conv_w attn_norm_g conv_norm_g w_out ln1_g ln1_b w_gate w_up w_down ln2_g ln2_b c_2 ada_w_2 "
    "ada_b_2 norm_g_2 ffn_w_in_2 ffn_w_down_2 attn_w_qkv_2 attn_w_o_2 attn_q_gain_2 attn_k_gain_2 attn_lambda_2 "
    "attn_subln_gain_2 rel_bias_2 hgrn_w_in_2 hgrn_w_o_2 hgrn_out_gain_2 hgrn_lb_logits_2"
).split()


def kernel(**inputs):
    import concourse.bacc as bacc
    from concourse.bass_utils import run_bass_kernel_spmd

    nc = bacc.Bacc("TRN2", target_bir_lowering=False, num_devices=1)
    arrays, args = {}, []
    for name in INPUTS:
        a = np.ascontiguousarray(inputs[name])
        arrays[f"in_{name}"] = a
        args.append(nc.dram_tensor(f"in_{name}", a.shape, mybir.dt.from_np(a.dtype), kind="ExternalInput").ap())
    args.append(nc.dram_tensor("out_x", (1, TOK, D), F32, kind="ExternalOutput").ap())
    two_blocks(nc, *args)
    r = run_bass_kernel_spmd(nc, [arrays], core_ids=[0])
    return r.results[0]["out_x"]
```

```python
import math
from contextlib import ExitStack

import concourse.bass as bass
import numpy as np
from concourse import mybir

F32 = mybir.dt.float32
F32R = mybir.dt.float32r
U8 = mybir.dt.uint8
ALU = mybir.AluOpType
ACT = mybir.ActivationFunctionType
AX = mybir.AxisListType

P = 128
TOK = 256
NT = TOK // P
D = 1024
KT = D // P
FF = 2816
FC = 256
NCH = FF // FC
BANK = 512
UNIT = 2048
RING = 3
NSUB = 8
HEADS = 8
ALPHA = 2.0 ** 0.25
EPS1, EPS2 = 1e-5, 1e-6
NEG = -1e30
AW = 512
TOKC = 936
KO, VO, QIO, KIO, WIO = 512, 576, 640, 896, 928
TOPK = 64
IDX_SCALE = 8 ** -0.5 * 32 ** -0.5
BUCKETS = 32
LAMBDA_INIT = 0.8 - 0.6 * math.exp(0.0)
TOE = 384
CHUNK = 64
LEVELS = (64, 32, 16, 8, 4, 2, 1)

V_C, V_C2, V_NORM, V_AG, V_CG, V_CW, V_OG, V_LB, V_QG, V_KG, V_SG = 0, 8, 16, 64, 68, 72, 84, 92, 100, 101, 102
NVEC = 103
PRE = KT
UNITS = (14, 33, 33, 16, 33, 33, 20, 33)
FIRST = tuple(PRE + sum(UNITS[:s]) for s in range(NSUB + 1))
SWIGLUS = (1, 2, 4, 5, 7)
SUMS = {0: 5, 1: 2, 3: 10, 6: 2}
LN_ROOT, ATT_ROOT, QK_ROOT = {0: 3, 1: 5}, {0: 1, 3: 19, 6: 27}, 11
RMS_ROOT = {1: 7, 2: 9, 3: 21, 4: 23, 5: 25, 6: 29}
COL_BANK = 5
HGRN_BLOCKS = (1024, 1536, 0, 512, 2048, 2560, 3072, 3584)
AHEAD = {
    0: ((1, 0), (1, 1)), 1: ((1, 2), (2, 0), (2, 1), (2, 2)), 2: ((3, 0), (3, 1), (3, 2), (4, 0), (4, 1)),
    4: ((4, 2), (5, 0), (5, 1), (5, 2)), 5: ((6, 0), (6, 1), (6, 2), (7, 0), (7, 1)), 7: ((7, 2),),
}
LATE_GATES = (1, 4, 7)
ADA_SLOTS = 3


def pieces_before(s, slot=None):
    own = KT if slot is None else len(range(slot, KT, ADA_SLOTS)) if slot < ADA_SLOTS else 0
    return own + sum(KT * (len(v) if slot is None else int(slot < len(v))) for k, v in AHEAD.items() if k < s)


def first_pieces(s):
    seen = {a for k, v in AHEAD.items() if k < s for a, _ in v}
    return sorted({a for a, _ in AHEAD[s]} - seen)


def pieces_until(s, j):
    return pieces_before(next(k for k, v in AHEAD.items() if (s, j) in v) + 1)


def sums_before(s):
    return sum(n for k, n in SUMS.items() if k < s)


def gate_bank(s):
    return 2 if s == 0 else 4 if s in LATE_GATES else 6


def shape_constants():
    f = np.float32
    ident = np.eye(P, dtype=f)
    q, k = np.arange(P)[:, None], np.arange(TOK)[None, :]
    causal = np.where(k > q + P, f(NEG), f(0)).astype(f)
    inv = f(500000.0) ** (-(np.arange(0, 16, 2, dtype=f) / f(16)))
    ang = np.arange(TOK, dtype=f)[:, None] * inv[None, :].astype(f)
    cos = np.cos(ang).astype(f).reshape(NT, P, 8).transpose(1, 0, 2).reshape(P, 16)
    sin = np.sin(ang).astype(f).reshape(NT, P, 8).transpose(1, 0, 2).reshape(P, 16)
    half = (np.arange(P)[:, None] // 64 == np.arange(2)[None, :]).astype(f)
    consts = np.concatenate([ident, causal, cos, sin, half], axis=1)
    spread = (np.arange(8)[:, None] == (np.arange(AW)[None, :] // 64)).astype(f)
    dist = 255 - np.arange(TOE)
    d_f = np.maximum(dist, 1).astype(f)
    large = 16 + (np.log(d_f / f(16)) / f(math.log(128 / 16)) * f(16)).astype(np.int32)
    bucket = np.where(dist < 16, np.maximum(dist, 0), np.minimum(large, BUCKETS - 1))
    bucket = np.where(dist < 0, BUCKETS, bucket)
    onehot = (np.arange(BUCKETS + 1)[:, None] == bucket[None, :]).astype(f)
    s, t = np.arange(P)[:, None], np.arange(P)[None, :]
    masks = [s == t] + [(s // (2 * n) == t // (2 * n)) & (s % (2 * n) < n) & (t % (2 * n) >= n) for n in LEVELS]
    return consts, spread, onehot, np.stack(masks, 1).astype(np.uint8)


C_ID, C_CAUSAL, C_COS, C_SIN, C_HALF, C_END = 0, 128, 384, 400, 416, 418


def two_blocks(
    nc, x, c, w_ada, b_ada, w_in, conv_w, attn_norm_g, conv_norm_g, w_out, ln1_g, ln1_b, w_gate,
    w_up, w_down, ln2_g, ln2_b, c_2, ada_w_2, ada_b_2, norm_g_2, ffn_w_in_2, ffn_w_down_2,
    attn_w_qkv_2, attn_w_o_2, attn_q_gain_2, attn_k_gain_2, attn_lambda_2, attn_subln_gain_2,
    rel_bias_2, hgrn_w_in_2, hgrn_w_o_2, hgrn_out_gain_2, hgrn_lb_logits_2, out,
):
    consts, spread, onehot, masks = (
        nc.inline_tensor(a, name=n).ap() for a, n in
        zip(shape_constants(), ("shape_consts", "group_spread", "bucket_onehot", "level_masks")))
    bias_rows = nc.dram_tensor("bias_rows", (P, HEADS, TOE), F32, kind="Internal").ap()

    def ada_weight(s):
        w = w_ada[0] if s < 2 else ada_w_2[(s - 2) // 3]
        first = (s if s < 2 else (s - 2) % 3) * 3 * D
        return w, first

    def ada_bias(s):
        b = b_ada[0:1] if s < 2 else ada_b_2[(s - 2) // 3:(s - 2) // 3 + 1]
        first = (s if s < 2 else (s - 2) % 3) * 3 * D
        return b[:, first:first + 3 * D]

    def swiglu_weights(s):
        if s == 1:
            return w_gate[0], w_up[0], w_down[0]
        layer, which = ((0, 0), (0, 1), (1, 0), (1, 1))[(2, 4, 5, 7).index(s)]
        w = ffn_w_in_2[layer, which]
        return w[:, 0:FF], w[:, FF:2 * FF], ffn_w_down_2[layer, which]

    with ExitStack() as ctx:
        def sb(name, shape, dt=F32):
            return ctx.enter_context(nc.sbuf_tensor(name, shape, dt))

        def sem(name):
            return ctx.enter_context(nc.semaphore(name))

        raw = sb("raw", [P, RING, UNIT])
        whi = sb("whi", [P, RING, UNIT], F32R)
        wlo = sb("wlo", [P, RING, UNIT], F32R)
        ada_raw = sb("ada_raw", [P, 3, D])
        ada_acc = sb("ada_acc", [P, 2, 3 * D])
        xs = sb("xs", [P, NT, D])
        xn = sb("xn", [P, NT, D])
        hf = sb("hf", [P, KT, TOK])
        hhi = sb("hhi", [P, KT, TOK], F32R)
        hlo = sb("hlo", [P, KT, TOK], F32R)
        gate = sb("gate", [P, 2, D])
        act = sb("act", [P, NT, FC])
        ahi = sb("ahi", [P, 2, TOK], F32R)
        alo = sb("alo", [P, 2, TOK], F32R)
        big = sb("big", [P, 10240])
        kc = sb("kc", [P, C_END])
        ones = sb("ones", [P, P])
        vec = sb("vec", [P, NVEC])
        csil = sb("csil", [P, 16])
        modc = sb("modc", [P, 2, 16])
        mask8 = sb("mask8", [P, len(LEVELS) + 1, P], U8)
        st = sb("st", [P, 256])
        ps = ctx.enter_context(nc.psum_tensor("ps", [P, 8, BANK], F32))
        psf = ps[:, :, :].rearrange("p b n -> p (b n)")

        ident = kc[:, C_ID:C_ID + P]
        half = st[:, 240:241]

        lam_rows = gate[:, 1, BANK:BANK + 256]

        qkv = big[:, 0:6144].rearrange("p (t n) -> p t n", t=NT)
        relb = big[:, 6144:8192].rearrange("p (h k) -> p h k", h=HEADS)
        soft = big[:, 8192:9216].rearrange("p (b c k) -> p b c k", b=2, c=2)
        weightsT = big[:, 9216:9728].rearrange("p (b n) -> p b n", b=2)
        qT, kT = xn[:, :, :].rearrange("p t (h n) -> p (t h) n", n=TOK), hf

        def by_head(flat):
            return flat.rearrange("p (h n) -> p h n", h=HEADS)

        h_q, h_k, h_G = (by_head(big[:, 2048 * n:2048 * (n + 1)]) for n in range(3))
        h_v, h_g = (big[:, 6144 + 2048 * n:8192 + 2048 * n].rearrange("p (t n) -> p t n", t=NT) for n in range(2))
        h_o = big[:, 0:2048].rearrange("p (t n) -> p t n", t=NT)
        scoresT = ada_acc[:, 0, :].rearrange("p (b n) -> p b n", n=P)
        chunk_carry = act[:, :, :].rearrange("p t n -> p (t n)")
        lb, one_less_lb = st[:, 224:232], st[:, 232:240]

        def decayed(level):
            return hf[:, :, :] if level % 2 else by_head(xn[:, :, :].rearrange("p t n -> p (t n)"))

        def halves(place, level):
            n = LEVELS[level - 1] if level <= len(LEVELS) else P
            return place.rearrange("p h (b a n) -> p (h b) a n", a=2, n=n)

        def bank(b, n=1):
            return psf[:, b * BANK:(b + n) * BANK]

        w_land = [sem(f"w_land{i}") for i in range(RING)]
        w_hi, w_lo, w_used = sem("w_hi"), sem("w_lo"), sem("w_used")
        a_land = [sem(f"a_land{i}") for i in range(5)]
        a_used = sem("a_used")
        acc_zero, acc_bias = sem("acc_zero"), sem("acc_bias")
        const_land, x_land, vec_land = sem("const_land"), sem("x_land"), sem("vec_land")
        ones_set, vec_tr, vec_set, csil_set = sem("ones_set"), sem("vec_tr"), sem("vec_set"), sem("csil_set")
        cols_sum, cols_set, gate_sum, gate_set = sem("cols_sum"), sem("cols_set"), sem("gate_sum"), sem("gate_set")
        h_src, h_tr, h_mod_v, h_mod_s, h_hi, h_lo = sem("h_src"), sem("h_tr"), sem("h_mod_v"), sem("h_mod_s"), sem("h_hi"), sem("h_lo")
        y_ready, x_new, root = sem("y_ready"), sem("x_new"), sem("root")
        gu_ready, silu_done, act_ready = sem("gu_ready"), sem("silu_done"), sem("act_ready")
        tr_ready, ahi_ready, alo_ready = sem("tr_ready"), sem("ahi_ready"), sem("alo_ready")
        mix_f, mix_hi, mix_lo = sem("mix_f"), sem("mix_hi"), sem("mix_lo")
        v_step, s_step = sem("v_step"), sem("s_step")
        ln_land, out_done = sem("ln_land"), sem("out_done")
        spread_land, mask_land, toe_land, lam_land = sem("spread_land"), sem("mask_land"), sem("toe_land"), sem("lam_land")
        sums_s, sums_v, root_in = sem("sums_s"), sem("sums_v"), sem("root_in")
        blk_ready, q_out, hc_out, rope_done, qk_tr = sem("blk_ready"), sem("q_out"), sem("hc_out"), sem("rope_done"), sem("qk_tr")
        qT_out, kT_out, idx_mm, relu_done, score_done = sem("qT_out"), sem("kT_out"), sem("idx_mm"), sem("relu_done"), sem("score_done")
        conv_u, conv_gated, conv_sq, group_mm = sem("conv_u"), sem("conv_gated"), sem("conv_sq"), sem("group_mm")
        group_tr, group_out, spread_mm = sem("group_tr"), sem("group_out"), sem("spread_mm")
        att_mm, max_done, exp_done, p_tr = sem("att_mm"), sem("max_done"), sem("exp_done"), sem("p_tr")
        pt_s, pt_v, pv_mm, o_done, o_tr = sem("pt_s"), sem("pt_v"), sem("pv_mm"), sem("o_done"), sem("o_tr")
        v_out, qk_sq, qk_out, qT3, kT3 = sem("v_out"), sem("qk_sq"), sem("qk_out"), sem("qT3"), sem("kT3")
        lam_dot, lam_exp, gains_set, dot_mm, sm_ready, sm_exp = sem("lam_dot"), sem("lam_exp"), sem("gains_set"), sem("dot_mm"), sem("sm_ready"), sem("sm_exp")
        a_ready, a_tr, aT_out, av_mm, head_sq = sem("a_ready"), sem("a_tr"), sem("aT_out"), sem("av_mm"), sem("head_sq")
        toe_fill, toe_mm, toe_rows, scan_set = sem("toe_fill"), sem("toe_mm"), sem("toe_rows"), sem("scan_set")
        lb_diff, lb_exp, f_neg, f_abs, f_log, f_taken, f_exp, k_ready = sem("lb_diff"), sem("lb_exp"), sem("f_neg"), sem("f_abs"), sem("f_log"), sem("f_taken"), sem("f_exp"), sem("k_ready")
        q_copied, vg_out, lv_sub, lv_exp, lv_mul = sem("q_copied"), sem("vg_out"), sem("lv_sub"), sem("lv_exp"), sem("lv_mul")
        lv_mm, lv_copy, g_silu = sem("lv_mm"), sem("lv_copy"), sem("g_silu")

        def linked(engine, own):
            count = [0]

            def link(instruction):
                count[0] += 1
                instruction.then_inc(own, 1)
                engine.wait_ge(own, count[0])
            return link

        def used(unit, lap=0):
            return unit - PRE + 1 + RING * lap

        def ring_view(ring, unit, k):
            return ring[:, unit % RING, :].rearrange("p (k n) -> p k n", k=k)

        def chunk_units(s, i):
            return FIRST[s] + 3 * i - 1 if i else FIRST[s], FIRST[s] + 3 * i if i else FIRST[s] + 1, FIRST[s] + 3 * i + 1

        def down_unit(s, i):
            return FIRST[s] + 3 * i + 4 if i < NCH - 1 else FIRST[s] + UNITS[s] - 1

        def split_places(final):
            return (hhi[:, 0:2, :], hlo[:, 0:2, :]) if final else (ahi[:, :, :], alo[:, :, :])

        def ada_slot(p):
            return ada_raw[:, p, :] if p < ADA_SLOTS else big[:, 8192 + (p - ADA_SLOTS) * D:8192 + (p - ADA_SLOTS + 1) * D]

        block = ctx.enter_context(nc.Block())

        @block.sync
        def _(sp):
            def load(unit, parts, lap=0):
                if unit >= RING:
                    sp.wait_ge(w_lo, unit - RING + 1 + RING * lap)
                for dst, src in parts:
                    sp.dma_start(dst, src).then_inc(w_land[unit % RING], 32 // len(parts))

            def rows(w, k0, k, c0, n):
                return w[k0 * P:(k0 + k) * P, c0:c0 + n].rearrange("(k p) n -> p k n", p=P)

            def load_block(unit, w, c0, n=BANK):
                for g in range(2):
                    dst = raw[:, (unit + g) % RING, 0:4 * n].rearrange("p (k n) -> p k n", k=4)
                    load(unit + g, [(dst, rows(w, 4 * g, 4, c0, n))])

            def load_out(unit, w, k0=0):
                for j in range(4):
                    load(unit + j, [(ring_view(raw, unit + j, 2), rows(w, (k0 + 2 * j) % KT, 2, 0, D))])

            w0, first = ada_weight(0)
            for kt in range(KT):
                load(kt, [(raw[:, kt % RING, :], w0[kt * P:(kt + 1) * P, first:first + 2 * D])])
                if kt == 5:
                    for t in range(NT):
                        sp.dma_start(xs[:, t, :], x[0, t * P:(t + 1) * P, :]).then_inc(x_land, 16)

            U = FIRST[0]
            load_block(U, w_in[0], 0)
            sp.dma_start(mask8[:, :, :], masks[:, :, :]).then_inc(mask_land, 16)
            sp.dma_start(lam_rows, attn_lambda_2.rearrange("a b n -> a (b n)").to_broadcast((P, 256)))\
                    .then_inc(lam_land, 16)
            load_block(U + 2, w_in[0], BANK, TOKC - BANK)
            for b, c0 in enumerate((TOKC + 2 * AW, TOKC + AW, TOKC)):
                load_block(U + 4 + 2 * b, w_in[0], c0)
            load_out(U + 10, w_out[0], 4)
            sp.wait_ge(vec_tr, 1)
            for n, row in enumerate((ln1_g, ln1_b)):
                sp.dma_start(big[:, n * D:(n + 1) * D], row.to_broadcast((P, D))).then_inc(ln_land, 16)

            def swiglu(s):
                g, u, d = swiglu_weights(s)

                def gate_up(unit, i, g0, lap=0):
                    slot = raw[:, unit % RING, :].rearrange("p (k h n) -> p k h n", k=4, h=2)
                    load(unit, [(slot[:, :, j, :],
                                 w[g0 * 4 * P:(g0 + 1) * 4 * P, bass.ds(i * FC, FC)].rearrange("(k p) n -> p k n", p=P))
                                for j, w in enumerate((g, u))], lap)

                def down(unit, i, lap=0):
                    load(unit, [(ring_view(raw, unit, 2),
                                 d[bass.ds(i * FC, FC), :].rearrange("(k p) n -> p k n", p=P))], lap)

                def body(units, i, lap=0):
                    gate_up(units[0], i, 0, lap)
                    gate_up(units[1], i, 1, lap)
                    down(units[2], i - 1, lap)

                gate_up(FIRST[s], 0, 0)
                gate_up(FIRST[s] + 1, 0, 1)
                body(chunk_units(s, 1), 1)
                with sp.Fori(2, NCH - 1) as i:
                    body(chunk_units(s, 2), i, i - 2)
                body(chunk_units(s, NCH - 1), NCH - 1)
                down(down_unit(s, NCH - 1), NCH - 1)

            for s in range(1, NSUB):
                if s in SWIGLUS:
                    swiglu(s)
                elif s == 3:
                    with sp.Fori(0, 2) as i:
                        for b in range(3):
                            for g in range(2):
                                unit = FIRST[3] + 2 * b + g
                                load(unit, [(ring_view(raw, unit, 4),
                                             attn_w_qkv_2[0][4 * g * P:4 * (g + 1) * P, bass.ds(b * D + i * BANK, BANK)]
                                             .rearrange("(k p) n -> p k n", p=P))], 2 * i)
                    load_out(FIRST[3] + 12, attn_w_o_2[0])
                else:
                    for b, c0 in enumerate(HGRN_BLOCKS):
                        load_block(FIRST[s] + 2 * b, hgrn_w_in_2[0], c0)
                    load_out(FIRST[s] + 16, hgrn_w_o_2[0])
                if s == 1:
                    sp.wait_ge(x_new, 2)
                    for n, row in enumerate((ln2_g, ln2_b)):
                        sp.dma_start(big[:, n * D:(n + 1) * D], row.to_broadcast((P, D))).then_inc(ln_land, 16)
            for t in range(NT):
                sp.wait_ge(x_new, 2 * (NSUB - 1) + t + 1)
                sp.dma_start(out[0, t * P:(t + 1) * P, :], xs[:, t, :]).then_inc(out_done, 16)
            sp.wait_ge(out_done, 32)

        @block.gpsimd
        def _(pool):
            def reciprocal_root(sums, value, col, width, n, eps):
                pool.wait_ge(sums, value)
                cols = st[:, col:col + width]
                pool.tensor_scalar(cols, cols, 1.0 / n, eps, ALU.mult, ALU.add).then_inc(root_in, 1)
                rooted[0] += 1
                pool.wait_ge(root_in, rooted[0])
                pool.tensor_tensor(cols, cols, half.to_broadcast((P, width)), ALU.pow).then_inc(root, 1)

            rooted = [0]

            def start_sums(s):
                if s >= 2:
                    pool.wait_ge(gate_sum, s - 1)
                pool.memset(ada_acc[:, s % 2, :], 0.0).then_inc(acc_zero, 1)
                pool.wait_ge(acc_zero, s + 1)
                pool.dma_start(ada_acc[0:1, s % 2, :], ada_bias(s)).then_inc(acc_bias, 16)

            def ada_pieces(s, kt0=0, kt1=KT):
                if kt0 == 0:
                    for a in first_pieces(s):
                        start_sums(a)
                base, m = pieces_before(s), len(AHEAD[s])
                pool.wait_ge(a_used, base)
                with pool.Fori(kt0, kt1) as kt:
                    for p, (a, j) in enumerate(AHEAD[s]):
                        w, first = ada_weight(a)
                        pool.wait_ge(a_used, base + p + 1 - m + m * kt)
                        pool.dma_start(ada_slot(p), w[bass.ds(kt * P, P), first + j * D:first + (j + 1) * D])\
                            .then_inc(a_land[p], 16)

            pool.memset(st[:, :], 0.0).then_inc(ones_set, 1)
            pool.wait_ge(ones_set, 1)
            pool.memset(half, -0.5).then_inc(ones_set, 1)
            pool.memset(ones[:, :], 1.0).then_inc(ones_set, 1)
            start_sums(0)
            pool.dma_start(gate[0:8, 1, 0:AW], spread[:, :]).then_inc(spread_land, 16)
            w0, first = ada_weight(0)
            pool.wait_ge(w_lo, KT - 1)
            for kt in range(KT):
                if kt >= ADA_SLOTS:
                    pool.wait_ge(a_used, kt - ADA_SLOTS + 1)
                pool.dma_start(ada_raw[:, kt % ADA_SLOTS, :], w0[kt * P:(kt + 1) * P, first + 2 * D:first + 3 * D])\
                    .then_inc(a_land[kt % ADA_SLOTS], 16)

            def rms_roots(s):
                for t in range(NT):
                    reciprocal_root(sums_s, 2 * (s - 1) + t + 1, t, 1, D, EPS2)

            def ln_roots(s):
                for t in range(NT):
                    reciprocal_root(sums_v, sums_before(s) + SUMS[s] - 1 + t, 5 + 2 * t, 1, 1, EPS1)

            for s in range(NSUB):
                if s in AHEAD:
                    if s == 1:
                        pool.wait_ge(x_new, 2)
                        pool.dma_start(big[0:BUCKETS + 1, 2048:2048 + TOE], onehot[:, :]).then_inc(toe_land, 16)
                        pool.memset(big[0:BUCKETS + 1, 2440:2448], NEG).then_inc(toe_fill, 1)
                        pool.wait_ge(toe_fill, 1)
                        pool.dma_start(big[0:BUCKETS, 2440:2448], rel_bias_2[:, :]).then_inc(toe_land, 16)
                        pool.wait_ge(toe_land, 32)
                        pool.tensor_copy(big[0:BUCKETS + 1, 2560:3584].rearrange("b (h q) -> b h q", h=HEADS),
                                         big[0:BUCKETS + 1, 2440:2448].unsqueeze(2).to_broadcast((BUCKETS + 1, HEADS, P)))\
                            .then_inc(toe_fill, 1)
                    ada_pieces(s, 0, KT if s else 3)
                if s == 0:
                    reciprocal_root(sums_v, 1, 40, 16, 64, EPS1)
                    for t in range(NT):
                        reciprocal_root(sums_v, 2 + t, 120 + 8 * t, 8, 64, EPS1)
                    ada_pieces(0, 3, KT)
                    ln_roots(0)
                elif s == 1:
                    pool.wait_ge(toe_rows, HEADS)
                    pool.dma_start(bias_rows[:, :, :], big[:, 3584:3584 + HEADS * TOE].rearrange("p (h j) -> p h j", h=HEADS))\
                        .then_inc(toe_land, 16)
                    pool.wait_ge(toe_land, 48)
                    skewed = bass.AP(tensor=bias_rows.tensor, offset=bias_rows.offset + P - 1,
                                     ap=[[HEADS * TOE - 1, P], [TOE, HEADS], [1, TOK]])
                    pool.dma_start(big[:, 6144:8192].rearrange("p (h k) -> p h k", h=HEADS), skewed)\
                        .then_inc(toe_land, 16)
                    ln_roots(1)
                if s == 3:
                    for n in range(8):
                        reciprocal_root(sums_v, sums_before(3) + n + 1, 152 + 8 * (n % 4), 8, 64, EPS2)
                    for t in range(NT):
                        reciprocal_root(sums_v, sums_before(3) + 9 + t, 120 + 8 * t, 8, P, EPS2)
                if s == 6:
                    pool.wait_ge(gate_sum, 7)
                    pool.memset(ada_acc[:, 0, :], 0.0).then_inc(scan_set, 1)
                    pool.wait_ge(w_used, used(FIRST[6] - 1))
                    flat = act[:, :, :].rearrange("p t n -> p (t n)")
                    pool.memset(flat, 1.0).then_inc(scan_set, 1)
                    pool.wait_ge(scan_set, 2)
                    pool.memset(flat[:, 0:2 * TOK:CHUNK], 0.0).then_inc(scan_set, 1)
                    for t in range(NT):
                        reciprocal_root(sums_v, sums_before(6) + 1 + t, 120 + 8 * t, 8, P, EPS2)
                if 1 <= s < NSUB - 1:
                    rms_roots(s)

        @block.scalar
        def _(sc):
            link = linked(sc, s_step)

            def hi(unit, lap=0, n=UNIT):
                slot, fill = unit % RING, unit // RING + 1
                sc.wait_ge(w_land[slot], 32 * fill + 32 * lap)
                if unit - PRE >= RING:
                    sc.wait_ge(w_used, used(unit - RING, lap))
                sc.activation(whi[:, slot, 0:n], raw[:, slot, 0:n], ACT.Copy).then_inc(w_hi, 1)

            def prefetch(s):
                for j in range(2):
                    hi(FIRST[s] + j)

            def split_inputs(s):
                sc.wait_ge(cols_set, s + 1)
                for t in range(NT):
                    sc.wait_ge(h_tr, 4 * s + 2 * t + 2)
                    for k in range(4):
                        kt = 4 + k
                        done = sc.activation(hf[:, kt, t * P:(t + 1) * P], ps[:, 2 * t + 1, k * P:(k + 1) * P], ACT.Identity,
                                             scale=modc[:, s % 2, 8 + kt:9 + kt], bias=modc[:, s % 2, kt:kt + 1])
                    done.then_inc(h_mod_s, 1)
                    for g, modulated in ((0, h_mod_v), (1, h_mod_s)):
                        sc.wait_ge(modulated, 2 * s + t + 1)
                        sc.activation(hhi[:, 4 * g:4 * g + 4, t * P:(t + 1) * P],
                                      hf[:, 4 * g:4 * g + 4, t * P:(t + 1) * P], ACT.Copy).then_inc(h_hi, 1)

            def split_mixed(n, k0, k, t0, tn):
                sc.wait_ge(mix_f, n)
                sc.activation(hhi[:, k0:k0 + k, t0:t0 + tn], hf[:, k0:k0 + k, t0:t0 + tn], ACT.Copy).then_inc(mix_hi, 1)

            def set_gate(s):
                sc.wait_ge(gate_sum, s + 1)
                sc.activation(gate[:, s % 2, :], bank(gate_bank(s), 2), ACT.Copy,
                              scale=1.0 if s in (0, 1, 3, 6) else 0.5).then_inc(gate_set, 1)

            def normalise(s):
                for t in range(NT):
                    sc.wait_ge(x_new, 2 * s + t + 1)
                    sc.activation(xn[:, t, :], xs[:, t, :], ACT.Square,
                                  accum_out=st[:, t:t + 1]).then_inc(sums_s, 1)
                    sc.wait_ge(root, RMS_ROOT[s] + t + 1)
                    sc.activation(xn[:, t, :], xs[:, t, :], ACT.Copy, scale=st[:, t:t + 1]).then_inc(h_src, 1)

            def swiglu(s):
                m = SWIGLUS.index(s) * NCH
                U = FIRST[s]

                def silu(i, unit, lap=0):
                    for t in range(NT):
                        if t == 0:
                            sc.wait_ge(gu_ready, m + i + 1)
                        else:
                            sc.wait_ge(w_used, used(unit, lap))
                        sc.activation(act[:, t, :], ps[:, 4 + t, 0:FC], ACT.Silu).then_inc(silu_done, 1)

                def ahi_of(i, final=False):
                    sc.wait_ge(tr_ready, m + i + 1)
                    sc.activation(split_places(final)[0].rearrange("p k n -> p (k n)"), bank(6), ACT.Copy).then_inc(ahi_ready, 1)

                def body(first, i, lap=0, more=True):
                    hi(first + 2, lap)
                    ahi_of(i - 1)
                    if more:
                        hi(first + 3, lap)
                    silu(i, first + 1, lap)
                    if more:
                        hi(first + 4, lap)

                hi(U + 2)
                silu(0, U + 1)
                hi(U + 3)
                body(U + 2, 1)
                if s == 1:
                    for h in range(HEADS):
                        sc.wait_ge(toe_mm, h + 1)
                        sc.activation(big[:, 3584 + h * TOE:3584 + (h + 1) * TOE], ps[:, 6 + h % 2, 0:TOE], ACT.Copy)\
                            .then_inc(toe_rows, 1)
                with sc.Fori(2, NCH - 1) as i:
                    body(U + 5, i, i - 2)
                body(U + 3 * (NCH - 1) - 1, NCH - 1, more=False)
                hi(U + UNITS[s] - 1)
                ahi_of(NCH - 1, final=True)

            def swiglu_end(s):
                if s in LATE_GATES:
                    set_gate(s)
                if s < NSUB - 1:
                    prefetch(s + 1)
                    normalise(s)

            def attention():
                U = FIRST[3]
                with sc.Fori(0, 2) as i:
                    hi(U + 2, 2 * i)
                    hi(U + 3, 2 * i)
                    for b in range(2):
                        for t in range(NT):
                            if t == 0:
                                sc.wait_ge(blk_ready, 2 + 3 * i + b + 1)
                            else:
                                sc.wait_ge(w_used, used(U + 2 * b + 1, 2 * i))
                            n = 2 * b + t
                            sc.activation(big[:, 8192 + n * BANK:8192 + (n + 1) * BANK], bank(2 * b + t), ACT.Square).then_inc(qk_sq, 1)
                        hi(U + 4 + 2 * b, 2 * i)
                        hi(U + 5 + 2 * b, 2 * i)
                    for t in range(NT):
                        if t == 0:
                            sc.wait_ge(blk_ready, 2 + 3 * i + 3)
                        else:
                            sc.wait_ge(w_used, used(U + 5, 2 * i))
                        sc.activation(qkv[:, t, bass.ds(2 * D + i * BANK, BANK)], bank(4 + t), ACT.Copy).then_inc(v_out, 1)
                    sc.wait_ge(qk_out, 4 * i + 4)
                for t in range(NT):
                    for g in range(2):
                        sc.wait_ge(qk_tr, 2 + 4 * t + 2 * g + 1)
                        sc.activation(qT[:, 4 * g:4 * g + 4, t * P:(t + 1) * P],
                                      bank(4 * t + 2 * g).rearrange("p (h n) -> p h n", h=4), ACT.Copy,
                                      scale=st[:, 216:217]).then_inc(qT3, 1)

                def softmax(i):
                    t, keys = i // HEADS, P * (i // HEADS + 1)
                    sc.wait_ge(sm_ready, i + 1)
                    for c in range(2):
                        p = soft[:, i % 2, c, 0:keys]
                        done = sc.activation(p, p, ACT.Exp, bias=st[:, 88 + 2 * (i % 2) + c:89 + 2 * (i % 2) + c],
                                             accum_out=st[:, 72 + 2 * (i % 2) + c:73 + 2 * (i % 2) + c])
                    done.then_inc(sm_exp, 1)

                def take_weights(i):
                    keys = P * (i // HEADS + 1)
                    sc.wait_ge(a_tr, i + 1)
                    if i >= 2:
                        sc.wait_ge(av_mm, i - 1)
                    sc.activation(weightsT[:, i % 2, 0:keys], ps[:, 4 + i % 2, 0:keys], ACT.Copy).then_inc(aT_out, 1)

                def square_heads(t):
                    sc.wait_ge(av_mm, HEADS * (t + 1))
                    sc.activation(qkv[:, t, D:2 * D], bank(6, 2), ACT.Square).then_inc(head_sq, 1)

                for i in range(2 * HEADS):
                    if i == HEADS + 2:
                        square_heads(0)
                    softmax(i)
                    if i:
                        take_weights(i - 1)
                take_weights(2 * HEADS - 1)
                square_heads(1)
                for t in range(NT):
                    for g in range(2):
                        split_mixed(3 + 2 * t + g + 1, 4 * g, 4, t * P, P)
                hi(U + 14)
                hi(U + 15)
                prefetch(4)
                normalise(3)

            def hgrn():
                U = FIRST[6]
                flat_xn = xn[:, :, :].rearrange("p t n -> p (t n)")

                def forget(b):
                    e0 = flat_xn[:, b * D:(b + 1) * D]
                    sc.wait_ge(w_used, used(U + 2 * b + 1))
                    sc.activation(h_k[:, 4 * b:4 * b + 4, :], bank(2 * b, 2).rearrange("p (h n) -> p h n", h=4), ACT.Copy,
                                  scale=-1.0).then_inc(f_neg, 1)
                    hi(U + 4 + 3 * b)
                    sc.wait_ge(f_abs, b + 1)
                    if b == 0:
                        sc.wait_ge(lb_diff, 1)
                        sc.activation(st[:, 241:242], ones[:, 0:1], ACT.Ln)
                        sc.activation(lb, lb, ACT.Exp).then_inc(lb_exp, 1)
                    link(sc.activation(e0, e0, ACT.Exp))
                    sc.activation(e0, e0, ACT.Ln, bias=ones[:, 0:1]).then_inc(f_log, 1)
                    hi(U + 5 + 3 * b)
                    sc.wait_ge(f_taken, b + 1)
                    heads = slice(4 * b, 4 * b + 4)
                    sc.activation(h_k[:, heads, :], h_k[:, heads, :], ACT.Exp)
                    link(sc.activation(hf[:, heads, :], hf[:, heads, :], ACT.Exp, scale=-1.0))
                    sc.wait_ge(lb_diff, 2)
                    for h in range(4 * b, 4 * b + 4):
                        done = sc.activation(hf[:, h, :], hf[:, h, :], ACT.Ln, bias=ones[:, 0:1], scale=lb[:, h:h + 1])
                    done.then_inc(f_exp, 1)

                def take_queries(b):
                    sc.wait_ge(w_used, used(U + 5 + 2 * b))
                    sc.activation(h_q[:, 4 * b:4 * b + 4, :], bank(2 * b, 2).rearrange("p (h n) -> p h n", h=4), ACT.Copy)\
                        .then_inc(q_copied, 1)

                def exps(level):
                    E = decayed(level)
                    sc.wait_ge(lv_sub, level)
                    if level == 1:
                        e, g = halves(E, 1), halves(h_G, 1)
                        sc.activation(e[:, :, 0, :], e[:, :, 0, :], ACT.Exp)
                        done = sc.activation(e[:, :, 1, :], g[:, :, 1, :], ACT.Exp)
                    elif level <= len(LEVELS):
                        done = sc.activation(E, E, ACT.Exp)
                    else:
                        sc.activation(E[:, :, 0:P], E[:, :, 0:P], ACT.Exp)
                        sc.activation(E[:, :, P:P + CHUNK], h_G[:, :, P:P + CHUNK], ACT.Exp)
                        done = sc.activation(E[:, :, P + CHUNK:TOK], E[:, :, P + CHUNK:TOK], ACT.Exp)
                    done.then_inc(lv_exp, 1)

                def take_tokens(b):
                    for t in range(NT):
                        if t == 0:
                            sc.wait_ge(blk_ready, 8 + b + 1)
                        else:
                            sc.wait_ge(w_used, used(U + 9 + 2 * b))
                        dst = (h_v, h_g)[b // 2][:, t, (b % 2) * BANK:(b % 2 + 1) * BANK]
                        sc.activation(dst, bank(2 * (b % 2) + t), ACT.Copy).then_inc(vg_out, 1)

                hi(U + 2)
                hi(U + 3)
                forget(0)
                hi(U + 6)
                forget(1)
                take_queries(0)
                hi(U + 9)
                take_queries(1)
                hi(U + 10)
                for level in range(len(LEVELS) + 2):
                    if level <= 7:
                        hi(U + 11 + level)
                    if level <= len(LEVELS):
                        exps(level + 1)
                    if level % 2 and level <= 7:
                        take_tokens(level // 2)
                sc.wait_ge(vg_out, 8)
                sc.activation(h_g[:, :, :], h_g[:, :, :], ACT.Silu).then_inc(g_silu, 1)
                for t in range(NT):
                    sc.wait_ge(pv_mm, 2 + t + 1)
                    sc.activation(xn[:, t, :], bank(2 * t, 2), ACT.Square).then_inc(head_sq, 1)
                for t in range(NT):
                    for g in range(2):
                        split_mixed(7 + 2 * t + g + 1, 4 * g, 4, t * P, P)
                hi(U + 19)
                prefetch(7)
                normalise(6)

            sc.dma_start(kc[:, :], consts[:, :]).then_inc(const_land, 16)
            vrow = big
            for row, src in ((V_C, c), (V_C2, c_2), (V_AG, attn_norm_g), (V_CG, conv_norm_g),
                             (V_OG, hgrn_out_gain_2), (V_LB, hgrn_lb_logits_2)):
                n = src.shape[-1] // P
                sc.dma_start(vrow[row:row + n, 0:P], src.rearrange("a (k p) -> (a k) p", p=P)).then_inc(vec_land, 16)
            sc.dma_start(vrow[V_NORM:V_NORM + 48, 0:P],
                         norm_g_2.rearrange("l s (k p) -> (l s k) p", p=P)).then_inc(vec_land, 16)
            sc.dma_start(vrow[V_CW:V_CW + 12, 0:P],
                         conv_w[0].rearrange("j (k p) -> (j k) p", p=P)).then_inc(vec_land, 16)
            for row, src in ((V_QG, attn_q_gain_2), (V_KG, attn_k_gain_2)):
                for c0 in (0, 64):
                    sc.dma_start(vrow[row:row + 1, c0:c0 + 64], src[:, :]).then_inc(vec_land, 16)
            sc.dma_start(vrow[V_SG:V_SG + 1, 0:P], attn_subln_gain_2[:, :]).then_inc(vec_land, 16)
            sc.wait_ge(vec_land, 208)
            sc.wait_ge(vec_set, 1)
            sc.activation(csil[:, :], vec[:, V_C:V_C + 16], ACT.Silu).then_inc(csil_set, 1)
            U = FIRST[0]
            n_b = 4 * (TOKC - BANK)
            hi(U)
            split_inputs(0)
            hi(U + 1)
            hi(U + 2, n=n_b)
            tok = big[:, 2048:2048 + NT * TOKC].rearrange("p (t n) -> p t n", t=NT)
            L = big[:, 3920:5968].rearrange("p (h k) -> p h k", h=HEADS)
            PT = big[:, 5968:8016].rearrange("p (g n) -> p g n", g=2)
            hi(U + 3, n=n_b)
            sc.wait_ge(blk_ready, 1)
            sc.activation(tok[:, 0, 0:BANK], bank(4), ACT.Copy).then_inc(q_out, 1)
            sc.wait_ge(w_used, used(U + 1))
            sc.activation(tok[:, 1, 0:BANK], bank(5), ACT.Copy).then_inc(q_out, 1)
            hi(U + 4)
            hi(U + 5)
            hi(U + 6)
            hi(U + 7)
            sc.wait_ge(w_used, used(U + 5))
            hfl = hf[:, :, :].rearrange("p k n -> p (k n)")
            xfl = xn[:, :, :].rearrange("p t n -> p (t n)")
            sc.wait_ge(h_lo, 4)
            sc.activation(hfl[:, 0:D], bank(0, 2), ACT.Copy).then_inc(hc_out, 1)
            sc.wait_ge(qk_tr, 1)
            sc.activation(xfl[:, 0:D], bank(4, 2), ACT.Copy).then_inc(qT_out, 1)
            for t in range(NT):
                hi(U + 8 + t)
                keys = P * (t + 1)
                sc.wait_ge(idx_mm, t + 1)
                if t:
                    sc.wait_ge(score_done, t)
                for r in range(4):
                    ins = ps[:, 4 + r, 0:2 * keys].rearrange("p (j k) -> p j k", j=2)
                    outs = L.rearrange("p (j r) k -> p j r k", r=4)[:, :, r, 0:keys]
                    done = sc.activation(outs, ins, ACT.Relu)
                done.then_inc(relu_done, 1)
            hi(U + 10)
            sc.wait_ge(lam_dot, 1)
            sc.activation(st[:, 218:220], st[:, 218:220], ACT.Exp).then_inc(lam_exp, 1)
            for t in range(NT):
                keys = P * (t + 1)
                sc.wait_ge(max_done, t + 1)
                for h in range(HEADS):
                    done = sc.activation(L[:, h, 0:keys], L[:, h, 0:keys], ACT.Exp, bias=st[:, 88 + h:89 + h],
                                            accum_out=st[:, 72 + 8 * t + h:73 + 8 * t + h])
                done.then_inc(exp_done, 1)
                if t:
                    sc.wait_ge(conv_gated, 1)
                    sc.activation(hfl[:, 0:D], hfl[:, D:2 * D], ACT.Square).then_inc(conv_sq, 1)
                else:
                    set_gate(0)
                    hi(U + 11)
                sc.wait_ge(p_tr, t + 1)
                sc.activation(PT[:, 0, :], bank(4, 2), ACT.Copy).then_inc(pt_s, 1)
            sc.wait_ge(group_tr, 1)
            sc.activation(act[0:8, 0, 0:TOK], ps[0:8, 1, 0:TOK], ACT.Copy).then_inc(group_out, 1)
            split_mixed(1, 4, 4, 0, TOK)
            for t in range(NT):
                split_mixed(2 + t, 0, 4, t * P, P)
            hi(U + 12)
            hi(U + 13)
            prefetch(1)

            for s in range(1, NSUB):
                split_inputs(s)
                if s not in LATE_GATES:
                    set_gate(s)
                if s in SWIGLUS:
                    swiglu(s)
                    swiglu_end(s)
                elif s == 3:
                    attention()
                else:
                    hgrn()

        @block.vector
        def _(ve):
            link = linked(ve, v_step)

            def lo(unit, lap=0, n=UNIT):
                slot = unit % RING
                ve.wait_ge(w_hi, used(unit, lap))
                ve.tensor_tensor(wlo[:, slot, 0:n], raw[:, slot, 0:n], whi[:, slot, 0:n].bitcast(F32), ALU.subtract)\
                    .then_inc(w_lo, 1)

            def prefetch(s):
                for j in range(2):
                    lo(FIRST[s] + j)

            def ada(s, pieces, kt):
                if not pieces:
                    return
                base, m = pieces_before(s), len(AHEAD[s])
                for p in pieces:
                    a, j = AHEAD[s][p]
                    ve.wait_ge(acc_bias, 16 * (max(b for b, _ in AHEAD[s]) + 1))
                    ve.wait_ge(a_land[p], 16 * (pieces_before(s, p) + 1) + 16 * kt)
                    ve.wait_ge(a_used, base + p - m + 1 + m * kt)
                    acc = ada_acc[:, a % 2, j * D:(j + 1) * D]
                    ve.scalar_tensor_tensor(acc, ada_slot(p), csil[:, bass.ds((0 if a < 2 else 8) + kt, 1)], acc,
                                            ALU.mult, ALU.add).then_inc(a_used, 1)

            def set_columns(s):
                par = s % 2
                ve.wait_ge(cols_sum, s + 1)
                link(ve.tensor_copy(modc[:, par, 0:8], ps[:, COL_BANK, 0:8]))
                if s < 2:
                    ve.tensor_scalar(modc[:, par, 8:16], ps[:, COL_BANK, 8:16], 1.0, None, ALU.add).then_inc(cols_set, 1)
                else:
                    g = V_NORM + 8 * (s - 2)
                    ve.scalar_tensor_tensor(modc[:, par, 8:16], ps[:, COL_BANK, 8:16], 1.0, vec[:, g:g + 8],
                                            ALU.add, ALU.mult).then_inc(cols_set, 1)

            def split_inputs(s):
                par = s % 2
                ve.wait_ge(cols_set, s + 1)
                for t in range(NT):
                    ve.wait_ge(h_tr, 4 * s + 2 * t + 1)
                    for kt in range(4):
                        done = ve.tensor_scalar(hf[:, kt, t * P:(t + 1) * P], ps[:, 2 * t, kt * P:(kt + 1) * P],
                                                modc[:, par, 8 + kt:9 + kt], modc[:, par, kt:kt + 1], ALU.mult, ALU.add)
                    done.then_inc(h_mod_v, 1)
                    for g in range(2):
                        ve.wait_ge(h_hi, 4 * s + 2 * t + g + 1)
                        part = (slice(None), slice(4 * g, 4 * g + 4), slice(t * P, (t + 1) * P))
                        ve.tensor_tensor(hlo[part], hf[part], hhi[part].bitcast(F32), ALU.subtract).then_inc(h_lo, 1)
                    if s == 0 and t == 0:
                        lo(FIRST[0])

            def split_mixed(n, k0, k, t0, tn):
                ve.wait_ge(mix_hi, n)
                part = (slice(None), slice(k0, k0 + k), slice(t0, t0 + tn))
                ve.tensor_tensor(hlo[part], hf[part], hhi[part].bitcast(F32), ALU.subtract).then_inc(mix_lo, 1)

            def finish(s):
                ve.wait_ge(gate_set, s + 1)

                def gated(t):
                    if t == 0:
                        ve.wait_ge(y_ready, s + 1)
                    else:
                        ve.wait_ge(w_used, used(FIRST[s + 1] - 1))
                    link(ve.tensor_tensor(xn[:, t, :], bank(2 * t, 2), gate[:, s % 2, :], ALU.mult))

                def moments(t):
                    link(ve.scalar_tensor_tensor(xs[:, t, :], xs[:, t, :], ALPHA, xn[:, t, :], ALU.mult, ALU.add))
                    stats = st[:, 12 + 12 * t:24 + 12 * t]
                    for g in range(2):
                        link(ve.bn_stats(stats[:, 6 * g:6 * g + 6], xs[:, t, g * BANK:(g + 1) * BANK]))
                    ve.bn_aggr(st[:, 4 + 2 * t:6 + 2 * t], stats).then_inc(sums_v, 1)

                def layer_norm(t):
                    ve.wait_ge(root, LN_ROOT[s] + t + 1)
                    link(ve.scalar_tensor_tensor(xs[:, t, :], xs[:, t, :], st[:, 4 + 2 * t:5 + 2 * t], big[:, 0:D],
                                                 ALU.subtract, ALU.mult))
                    ve.scalar_tensor_tensor(xs[:, t, :], xs[:, t, :], st[:, 5 + 2 * t:6 + 2 * t], big[:, D:2 * D],
                                            ALU.mult, ALU.add).then_inc(x_new, 1)

                if s >= 2:
                    for t in range(NT):
                        gated(t)
                        ve.tensor_tensor(xs[:, t, :], xs[:, t, :], xn[:, t, :], ALU.add).then_inc(x_new, 1)
                    return
                gated(0)
                moments(0)
                gated(1)
                ve.wait_ge(ln_land, 32 * (s + 1))
                layer_norm(0)
                moments(1)
                layer_norm(1)

            def conclude(s):
                finish(s)
                if s < NSUB - 1:
                    lo(FIRST[s + 1])
                    set_columns(s + 1)

            def swiglu(s):
                m = SWIGLUS.index(s) * NCH
                U = FIRST[s]
                count = len(AHEAD.get(s, ()))

                def multiply(i):
                    for t in range(NT):
                        ve.wait_ge(silu_done, 2 * (m + i) + t + 1)
                        ve.tensor_tensor(act[:, t, :], act[:, t, :], ps[:, 4 + t, FC:2 * FC], ALU.mult).then_inc(act_ready, 1)

                def alo_of(i, final=False):
                    ve.wait_ge(ahi_ready, m + i + 1)
                    a_hi, a_lo = (a.rearrange("p k n -> p (k n)") for a in split_places(final))
                    ve.tensor_tensor(a_lo, bank(6), a_hi.bitcast(F32), ALU.subtract).then_inc(alo_ready, 1)

                def body(first, i, lap=0, more=True, kt=None):
                    pieces = range(count) if kt is not None else ()
                    lo(first + 2, lap)
                    alo_of(i - 1)
                    ada(s, pieces[:count // 2], kt)
                    if more:
                        lo(first + 3, lap)
                    multiply(i)
                    if more:
                        lo(first + 4, lap)
                    ada(s, pieces[count // 2:], kt)

                lo(U + 2)
                multiply(0)
                lo(U + 3)
                body(U + 2, 1)
                with ve.Fori(2, NCH - 1) as i:
                    body(U + 5, i, i - 2, kt=i - 2 if count else None)
                body(U + 3 * (NCH - 1) - 1, NCH - 1, more=False)
                lo(U + UNITS[s] - 1)
                alo_of(NCH - 1, final=True)
                conclude(s)

            ve.wait_ge(vec_tr, 1)
            ve.tensor_copy(vec[:, :], ps[:, 0, 0:NVEC]).then_inc(vec_set, 1)
            ve.wait_ge(csil_set, 1)
            ve.wait_ge(acc_bias, 16)
            for kt in range(KT):
                ve.wait_ge(w_land[kt % RING], 32 * (kt // RING + 1))
                if kt:
                    ve.wait_ge(w_lo, kt)
                ve.scalar_tensor_tensor(ada_acc[:, 0, 0:2 * D], raw[:, kt % RING, :], csil[:, kt:kt + 1],
                                        ada_acc[:, 0, 0:2 * D], ALU.mult, ALU.add).then_inc(w_lo, 1)
            set_columns(0)
            split_inputs(0)
            U = FIRST[0]
            n_b = 4 * (TOKC - BANK)
            lo(U + 1)
            lo(U + 2, n=n_b)
            ve.wait_ge(lam_land, 16)
            lam = lam_rows.rearrange("p (a b n) -> p a b n", a=2, b=2)
            link(ve.tensor_tensor(lam[:, :, 0, :], lam[:, :, 0, :], lam[:, :, 1, :], ALU.mult))
            ve.tensor_reduce(st[:, 218:220], lam[:, :, 0, :], axis=AX.X, op=ALU.add).then_inc(lam_dot, 1)
            ve.tensor_scalar(st[:, 216:217], vec[:, V_QG:V_QG + 1], 64 ** -0.5, None, ALU.mult).then_inc(gains_set, 1)
            ve.tensor_scalar(st[:, 217:218], vec[:, V_SG:V_SG + 1], 1.0 - LAMBDA_INIT, None, ALU.mult).then_inc(gains_set, 1)

            def own_gate(kt):
                ve.wait_ge(a_land[kt % ADA_SLOTS], 16 * (kt // ADA_SLOTS + 1))
                if kt:
                    ve.wait_ge(a_used, kt)
                acc = ada_acc[:, 0, 2 * D:3 * D]
                ve.scalar_tensor_tensor(acc, ada_raw[:, kt % ADA_SLOTS, :], csil[:, kt:kt + 1], acc, ALU.mult, ALU.add)\
                    .then_inc(a_used, 1)

            own_gate(0)
            own_gate(1)
            lo(U + 3, n=n_b)
            own_gate(2)
            own_gate(3)
            lo(U + 4)
            for kt in range(4, 8):
                own_gate(kt)
            tok = big[:, 2048:2048 + NT * TOKC].rearrange("p (t n) -> p t n", t=NT)
            L = big[:, 3920:5968].rearrange("p (h k) -> p h k", h=HEADS)
            PT = big[:, 5968:8016].rearrange("p (g n) -> p g n", g=2)
            hfl = hf[:, :, :].rearrange("p k n -> p (k n)")
            xfl = xn[:, :, :].rearrange("p t n -> p (t n)")

            def ada1(kt):
                ada(0, range(2), kt)

            for t in range(NT):
                if t == 0:
                    ve.wait_ge(blk_ready, 2)
                else:
                    ve.wait_ge(w_used, used(U + 3))
                link(ve.tensor_copy(tok[:, t, BANK:TOKC], ps[:, 6 + t, 0:TOKC - BANK]))
            ve.wait_ge(q_out, 2)
            lo(U + 5)
            scr = big[:, 8016:8016 + 4 * 144].rearrange("p (m t h n) -> p m t h n", m=4, t=NT, h=9)
            cos = kc[:, C_COS:C_COS + 16].rearrange("p (t n) -> p t n", t=NT).unsqueeze(2).to_broadcast((P, NT, 9, 8))
            sin = kc[:, C_SIN:C_SIN + 16].rearrange("p (t n) -> p t n", t=NT).unsqueeze(2).to_broadcast((P, NT, 9, 8))
            for c0, w in ((0, 64), (QIO, 32)):
                heads = tok[:, :, c0:c0 + 9 * w].rearrange("p t (h n) -> p t h n", h=9)
                x1, x2 = heads[:, :, :, 0:8], heads[:, :, :, 8:16]
                for n, (a, b) in enumerate(((x1, cos), (x2, sin), (x2, cos), (x1, sin))):
                    link(ve.tensor_tensor(scr[:, n], a, b, ALU.mult))
                link(ve.tensor_tensor(x1, scr[:, 0], scr[:, 1], ALU.subtract))
                link(ve.tensor_tensor(x2, scr[:, 2], scr[:, 3], ALU.add))
            kk = big[:, 8592:8848].rearrange("p (t r n) -> p t r n", t=NT, r=2)
            ki4 = big[:, 8848:9104].rearrange("p (t r n) -> p t r n", t=NT, r=4)
            link(ve.tensor_copy(kk, tok[:, :, KO:KO + 64].unsqueeze(2).to_broadcast((P, NT, 2, 64))))
            link(ve.tensor_scalar(tok[:, :, WIO:WIO + 8], tok[:, :, WIO:WIO + 8], IDX_SCALE, None, ALU.mult))
            ve.tensor_copy(ki4, tok[:, :, KIO:KIO + 32].unsqueeze(2).to_broadcast((P, NT, 4, 32))).then_inc(rope_done, 1)
            lo(U + 6)
            ve.wait_ge(qk_tr, 2)
            ve.tensor_copy(xfl[:, D:2 * D], bank(6, 2)).then_inc(kT_out, 1)
            lo(U + 7)
            ada1(0)
            u = hf[:, 4:8, :]
            cv = hf[:, 0:4, :]
            MARK = -3e38
            kill = big[:, 9104:9360]
            link(ve.tensor_scalar(kill, kc[:, C_CAUSAL:C_CAUSAL + TOK], NEG, None, ALU.add))
            allow = big[:, 9360:9872].rearrange("p (t k) -> p t k", t=NT)
            top8 = st[:, 242:250]

            def scores(t):
                keys = P * (t + 1)
                off = TOK - keys
                score = allow[:, t, 0:keys]
                ve.wait_ge(relu_done, t + 1)
                link(ve.scalar_tensor_tensor(score, L[:, 0, 0:keys], tok[:, t, WIO:WIO + 1],
                                             kc[:, C_CAUSAL + off:C_CAUSAL + TOK], ALU.mult, ALU.add))
                for h in range(1, HEADS):
                    step = ve.scalar_tensor_tensor(score, L[:, h, 0:keys], tok[:, t, WIO + h:WIO + h + 1], score,
                                                   ALU.mult, ALU.add)
                    if h < HEADS - 1:
                        link(step)
                step.then_inc(score_done, 1)

            def choose(t):
                keys = P * (t + 1)
                score = allow[:, t, 0:keys]
                ve.wait_ge(score_done, t + 1)
                for n in range(TOPK // 8):
                    link(ve.max(top8, score))
                    link(ve.match_replace(score, top8, score, MARK))
                link(ve.tensor_scalar(score, score, MARK, -NEG, ALU.is_equal, ALU.mult))
                link(ve.tensor_tensor(score, score, kill[:, TOK - keys:TOK], ALU.add))
            def logits(t):
                keys = P * (t + 1)
                ve.wait_ge(att_mm, t + 1)
                if t:
                    ve.wait_ge(p_tr, t)
                mask = allow[:, t, 0:keys].unsqueeze(1).to_broadcast((P, 4, keys))
                for r in range(2):
                    ins = bank(4 + 2 * r, 2).rearrange("p (j k) -> p j k", j=4)[:, :, 0:keys]
                    link(ve.scalar_tensor_tensor(L[:, 4 * r:4 * r + 4, 0:keys], ins, 0.125, mask, ALU.mult, ALU.add))
                ve.tensor_reduce(st[:, 88:96], L[:, :, 0:keys], axis=AX.X, op=ALU.max, negate=True).then_inc(max_done, 1)

            def heads_out(t):
                O = ps[:, 2 + t, :]
                ob = big[:, 3920 + BANK * t:3920 + BANK * (t + 1)]
                sq = big[:, 3920 + BANK * (2 + t):3920 + BANK * (3 + t)]
                link(ve.reciprocal(st[:, 104 + 8 * t:112 + 8 * t], st[:, 72 + 8 * t:80 + 8 * t]))
                ve.wait_ge(pv_mm, t + 1)
                link(ve.tensor_tensor(ob.rearrange("p (j r d) -> p r j d", j=4, r=2), O.rearrange("p (r j d) -> p r j d", r=2, j=4),
                                      st[:, 104 + 8 * t:112 + 8 * t].rearrange("p (r j) -> p r j", r=2).unsqueeze(3)
                                      .to_broadcast((P, 2, 4, 64)), ALU.mult))
                link(ve.tensor_tensor(sq, ob, ob, ALU.mult))

            def sum_groups(t):
                sq = big[:, 3920 + BANK * (2 + t):3920 + BANK * (3 + t)]
                ve.tensor_reduce(st[:, 120 + 8 * t:128 + 8 * t], sq.rearrange("p (h d) -> p h d", h=HEADS), axis=AX.X, op=ALU.add)\
                    .then_inc(sums_v, 1)

            def heads_norm(t):
                ob = big[:, 3920 + BANK * t:3920 + BANK * (t + 1)].rearrange("p (h d) -> p h d", h=HEADS)
                ve.wait_ge(root, ATT_ROOT[0] + t + 1)
                ve.tensor_tensor(ob, ob, st[:, 120 + 8 * t:128 + 8 * t].unsqueeze(2).to_broadcast((P, HEADS, 64)), ALU.mult)\
                    .then_inc(o_done, 1)

            def pt_evac(t):
                if t:
                    ve.wait_ge(p_tr, t + 1)
                    ve.tensor_copy(PT[:, 1, :], bank(6, 2)).then_inc(pt_v, 1)

            scores(0)
            lo(U + 8)
            scores(1)
            ve.wait_ge(w_used, used(U + 7))
            ve.wait_ge(hc_out, 1)
            ve.tensor_tensor(hfl[:, D:2 * D], hfl[:, 0:D], bank(2, 2), ALU.mult).then_inc(conv_u, 1)
            lo(U + 9)
            choose(0)
            logits(0)
            choose(1)
            ada1(1)
            logits(1)
            ve.wait_ge(conv_u, 1)
            for ct in range(4):
                link(ve.tensor_scalar(cv[:, ct, :], u[:, ct, :], vec[:, V_CW + 8 + ct:V_CW + 9 + ct], None, ALU.mult))
                for j in (1, 2):
                    w = V_CW + 4 * (2 - j) + ct
                    link(ve.scalar_tensor_tensor(cv[:, ct, j:TOK], u[:, ct, 0:TOK - j], vec[:, w:w + 1], cv[:, ct, j:TOK],
                                                 ALU.mult, ALU.add))
            ve.wait_ge(w_used, used(U + 9))
            ve.tensor_tensor(hfl[:, D:2 * D], hfl[:, 0:D], bank(0, 2), ALU.mult).then_inc(conv_gated, 1)
            pt_evac(1)
            ve.wait_ge(group_mm, 1)
            ve.tensor_copy(st[:, 40:56], ps[:, 0, 0:16]).then_inc(sums_v, 1)
            heads_out(0)
            sum_groups(0)
            lo(U + 10)
            lo(U + 11)
            ada1(2)
            heads_out(1)
            sum_groups(1)
            ve.wait_ge(spread_mm, 1)
            link(ve.tensor_tensor(hfl[:, D:2 * D], hfl[:, D:2 * D], bank(0, 2), ALU.mult))
            ve.tensor_tensor(hf[:, 4:8, :], hf[:, 4:8, :], vec[:, V_CG:V_CG + 4].unsqueeze(2).to_broadcast((P, 4, TOK)), ALU.mult)\
                .then_inc(mix_f, 1)
            for t in range(NT):
                heads_norm(t)
            split_mixed(1, 4, 4, 0, TOK)
            for t in range(NT):
                ve.wait_ge(o_tr, t + 1)
                ve.tensor_tensor(hf[:, 0:4, t * P:(t + 1) * P], ps[:, 4 + t, :].rearrange("p (k n) -> p k n", k=4),
                                 vec[:, V_AG:V_AG + 4].unsqueeze(2).to_broadcast((P, 4, P)), ALU.mult).then_inc(mix_f, 1)
                split_mixed(2 + t, 0, 4, t * P, P)
            ve.wait_ge(lam_exp, 1)
            link(ve.tensor_tensor(st[:, 220:221], st[:, 219:220], st[:, 218:219], ALU.subtract))
            link(ve.tensor_scalar(st[:, 221:222], st[:, 220:221], -LAMBDA_INIT, None, ALU.add))
            ada1(3)
            lo(U + 12)
            ada1(4)
            ada1(5)
            lo(U + 13)
            ada1(6)
            ada1(7)
            conclude(0)

            def attention():
                U = FIRST[3]
                with ve.Fori(0, 2) as i:
                    lo(U + 2, 2 * i)
                    lo(U + 3, 2 * i)
                    for b in range(2):
                        for t in range(NT):
                            n = 2 * b + t
                            ve.wait_ge(qk_sq, 4 * i + n + 1)
                            ve.tensor_reduce(st[:, 152 + 8 * n:160 + 8 * n],
                                             big[:, 8192 + n * BANK:8192 + (n + 1) * BANK].rearrange("p (h d) -> p h d", h=8),
                                             axis=AX.X, op=ALU.add).then_inc(sums_v, 1)
                        lo(U + 4 + 2 * b, 2 * i)
                        for t in range(NT):
                            n = 2 * b + t
                            ve.wait_ge(root, QK_ROOT + 4 * i + n + 1)
                            ve.tensor_tensor(qkv[:, t, bass.ds(b * D + i * BANK, BANK)].rearrange("p (h d) -> p h d", h=8),
                                             bank(n).rearrange("p (h d) -> p h d", h=8),
                                             st[:, 152 + 8 * n:160 + 8 * n].unsqueeze(2).to_broadcast((P, 8, 64)), ALU.mult)\
                                .then_inc(qk_out, 1)
                        lo(U + 5 + 2 * b, 2 * i)
                for t in range(NT):
                    for g in range(2):
                        ve.wait_ge(qk_tr, 2 + 4 * t + 2 * g + 2)
                        ve.tensor_scalar(kT[:, 4 * g:4 * g + 4, t * P:(t + 1) * P],
                                         bank(4 * t + 2 * g + 1).rearrange("p (h n) -> p h n", h=4),
                                         vec[:, V_KG:V_KG + 1], None, ALU.mult).then_inc(kT3, 1)

                def add_bias(i):
                    t, h = divmod(i, HEADS)
                    keys = P * (t + 1)
                    ve.wait_ge(dot_mm, i + 1)
                    if t == 0 and i == 0:
                        ve.wait_ge(toe_land, 64)
                    s_ = soft[:, i % 2, :, 0:keys]
                    link(ve.tensor_tensor(s_, bank(2 * (i % 2), 2).rearrange("p (c k) -> p c k", c=2)[:, :, 0:keys],
                                          relb[:, h, TOK - keys:TOK].unsqueeze(1).to_broadcast((P, 2, keys)), ALU.add))
                    ve.tensor_reduce(st[:, 88 + 2 * (i % 2):90 + 2 * (i % 2)], s_, axis=AX.X, op=ALU.max, negate=True)\
                        .then_inc(sm_ready, 1)

                def combine(i):
                    keys = P * (i // HEADS + 1)
                    r = st[:, 104 + 2 * (i % 2):106 + 2 * (i % 2)]
                    ve.wait_ge(sm_exp, i + 1)
                    link(ve.reciprocal(r, st[:, 72 + 2 * (i % 2):74 + 2 * (i % 2)]))
                    link(ve.tensor_scalar(soft[:, i % 2, 1, 0:keys], soft[:, i % 2, 1, 0:keys], r[:, 1:2], st[:, 221:222],
                                          ALU.mult, ALU.mult))
                    ve.scalar_tensor_tensor(soft[:, i % 2, 0, 0:keys], soft[:, i % 2, 0, 0:keys], r[:, 0:1],
                                            soft[:, i % 2, 1, 0:keys], ALU.mult, ALU.add).then_inc(a_ready, 1)

                def sum_heads(t):
                    ve.wait_ge(head_sq, t + 1)
                    ve.tensor_reduce(st[:, 120 + 8 * t:128 + 8 * t], qkv[:, t, D:2 * D].rearrange("p (h d) -> p h d", h=HEADS),
                                     axis=AX.X, op=ALU.add).then_inc(sums_v, 1)

                def norm_heads(t):
                    ve.wait_ge(root, ATT_ROOT[3] + t + 1)
                    ve.tensor_tensor(qkv[:, t, 0:D].rearrange("p (h d) -> p h d", h=HEADS),
                                     bank(6, 2).rearrange("p (h d) -> p h d", h=HEADS),
                                     st[:, 120 + 8 * t:128 + 8 * t].unsqueeze(2).to_broadcast((P, HEADS, P)), ALU.mult)\
                        .then_inc(o_done, 1)

                for i in range(2 * HEADS):
                    if i >= 2:
                        ve.wait_ge(a_tr, i - 1)
                    if i == HEADS + 3:
                        norm_heads(0)
                    add_bias(i)
                    if i == HEADS + 2:
                        sum_heads(0)
                    if i:
                        combine(i - 1)
                combine(2 * HEADS - 1)
                sum_heads(1)
                norm_heads(1)
                for t in range(NT):
                    for g in range(2):
                        n = 2 * t + g
                        ve.wait_ge(o_tr, 2 + n + 1)
                        ve.tensor_scalar(hf[:, 4 * g:4 * g + 4, t * P:(t + 1) * P], bank(n).rearrange("p (k n) -> p k n", k=4),
                                         st[:, 217:218], None, ALU.mult).then_inc(mix_f, 1)
                        if n:
                            g1, t1 = (n - 1) % 2, (n - 1) // 2
                            split_mixed(3 + n, 4 * g1, 4, t1 * P, P)
                split_mixed(7, 4, 4, P, P)
                lo(U + 14)
                lo(U + 15)
                conclude(3)

            def hgrn():
                U = FIRST[6]
                ve.tensor_tensor(lb, vec[:, V_LB:V_LB + 8], vec[:, V_LB:V_LB + 8], ALU.subtract).then_inc(lb_diff, 1)
                lo(U + 2)
                lo(U + 3)

                def forget(b):
                    heads = slice(4 * b, 4 * b + 4)
                    G, k, e1 = h_G[:, heads, :], h_k[:, heads, :], hf[:, heads, :]
                    f = bank(2 * b, 2).rearrange("p (h n) -> p h n", h=4)
                    e0 = xn[:, b, :].rearrange("p (h n) -> p h n", h=4)
                    ve.wait_ge(f_neg, b + 1)
                    ve.tensor_tensor(e0, k, f, ALU.min).then_inc(f_abs, 1)
                    lo(U + 4 + 3 * b)
                    ve.wait_ge(f_log, b + 1)
                    link(ve.scalar_tensor_tensor(G, f, 0.0, e0, ALU.min, ALU.subtract))
                    ve.tensor_tensor(k, G, k, ALU.add)
                    ve.tensor_scalar(e1, f, -80.0, None, ALU.max).then_inc(f_taken, 1)
                    lo(U + 5 + 3 * b)
                    if b == 0:
                        ve.wait_ge(lb_exp, 1)
                        link(ve.reciprocal(one_less_lb, lb))
                        link(ve.tensor_tensor(one_less_lb, lb, one_less_lb, ALU.mult))
                        link(ve.tensor_tensor(lb, one_less_lb, one_less_lb, ALU.subtract))
                        ve.tensor_scalar(one_less_lb, lb, -1.0, 1.0, ALU.mult, ALU.add).then_inc(lb_diff, 1)
                        ve.wait_ge(lb_diff, 2)
                    ve.wait_ge(f_exp, b + 1)
                    link(ve.tensor_tensor(G, G, e1, ALU.add))
                    ve.tensor_tensor(k, k, one_less_lb[:, heads].unsqueeze(2).to_broadcast((P, 4, TOK)), ALU.mult)
                    ve.wait_ge(scan_set, 3)
                    for h in range(0, 4, 2):
                        part = h_G[:, 4 * b + h:4 * b + h + 2, :].rearrange("p h n -> p (h n)")
                        done = ve.tensor_tensor_scan(part, chunk_carry, part, 0.0, ALU.mult, ALU.add)
                    done.then_inc(k_ready, 1)

                def differences(level):
                    E = decayed(level)
                    if level >= 3:
                        ve.wait_ge(lv_mm, 2 * (level - 1))
                    if level == 1:
                        ve.wait_ge(k_ready, 2)
                    if level <= len(LEVELS):
                        n = LEVELS[level - 1]
                        e, g = halves(E, level), halves(h_G, level)
                        middle = g[:, :, 0, n - 1:n].to_broadcast((P, HEADS * TOK // (2 * n), n))
                        done = ve.tensor_tensor(e[:, :, 0, :], middle, g[:, :, 0, :], ALU.subtract)
                        if level > 1:
                            done = ve.tensor_tensor(e[:, :, 1, :], g[:, :, 1, :], middle, ALU.subtract)
                    else:
                        e, g = (a.rearrange("p h (c n) -> p h c n", n=CHUNK) for a in (E, h_G))
                        total = [g[:, :, c, CHUNK - 1:CHUNK].to_broadcast((P, HEADS, CHUNK)) for c in range(3)]
                        link(ve.tensor_tensor(e[:, :, 0, :], total[0], g[:, :, 0, :], ALU.subtract))
                        ve.tensor_tensor(e[:, :, 0, :], e[:, :, 0, :], total[1], ALU.add)
                        ve.tensor_tensor(e[:, :, 1, :], total[1], g[:, :, 1, :], ALU.subtract)
                        done = ve.tensor_tensor(e[:, :, 3, :], g[:, :, 3, :], total[2], ALU.add)
                    done.then_inc(lv_sub, 1)

                def decay(level):
                    e, k, q = (halves(a, level) for a in (decayed(level), h_k, h_q))
                    ve.wait_ge(lv_exp, level)
                    ve.tensor_tensor(e[:, :, 0, :], e[:, :, 0, :], k[:, :, 0, :], ALU.mult)
                    if level == 1:
                        ve.wait_ge(q_copied, 2)
                    ve.tensor_tensor(e[:, :, 1, :], e[:, :, 1, :], q[:, :, 1, :], ALU.mult).then_inc(lv_mul, 1)

                def take_scores(level):
                    if level == 0:
                        ve.wait_ge(mask_land, 16)
                    for t in range(NT if level <= len(LEVELS) else 1):
                        ve.wait_ge(lv_mm, 2 * level + t + 1)
                        products = by_head(bank(4 + 2 * t, 2))
                        if level <= len(LEVELS):
                            if level:
                                ve.wait_ge(lv_copy, 2 * level - 1 + t)
                            done = ve.copy_predicated(scoresT[:, HEADS * t:HEADS * (t + 1), :],
                                                      mask8[:, level, :].unsqueeze(1).to_broadcast((P, HEADS, P)), products)
                        else:
                            done = ve.tensor_copy(scoresT[:, 2 * HEADS:3 * HEADS, :], products)
                        done.then_inc(lv_copy, 1)

                forget(0)
                lo(U + 6)
                forget(1)
                differences(1)
                lo(U + 9)
                lo(U + 10)
                for level in range(len(LEVELS) + 2):
                    if level:
                        decay(level)
                        take_scores(level - 1)
                        if level <= len(LEVELS):
                            differences(level + 1)
                    if level <= 7:
                        lo(U + 11 + level)
                take_scores(len(LEVELS) + 1)
                for t in range(NT):
                    ve.wait_ge(head_sq, 2 + t + 1)
                    ve.tensor_reduce(st[:, 120 + 8 * t:128 + 8 * t], xn[:, t, :].rearrange("p (h d) -> p h d", h=HEADS),
                                     axis=AX.X, op=ALU.add).then_inc(sums_v, 1)
                ve.wait_ge(g_silu, 1)
                for t in range(NT):
                    ve.wait_ge(root, ATT_ROOT[6] + t + 1)
                    o = h_o[:, t, :].rearrange("p (h d) -> p h d", h=HEADS)
                    link(ve.tensor_tensor(o, bank(2 * t, 2).rearrange("p (h d) -> p h d", h=HEADS),
                                          st[:, 120 + 8 * t:128 + 8 * t].unsqueeze(2).to_broadcast((P, HEADS, P)), ALU.mult))
                    ve.tensor_tensor(h_o[:, t, :], h_o[:, t, :], h_g[:, t, :], ALU.mult).then_inc(o_done, 1)
                for n in range(2 * NT + 1):
                    t, g = divmod(n, 2)
                    if n < 2 * NT:
                        ve.wait_ge(o_tr, 6 + n + 1)
                        ve.tensor_tensor(hf[:, 4 * g:4 * g + 4, t * P:(t + 1) * P], bank(n).rearrange("p (k n) -> p k n", k=4),
                                         vec[:, V_OG + 4 * g:V_OG + 4 * g + 4].unsqueeze(2).to_broadcast((P, 4, P)), ALU.mult)\
                            .then_inc(mix_f, 1)
                    if n:
                        split_mixed(7 + n, 4 * ((n - 1) % 2), 4, (n - 1) // 2 * P, P)
                lo(U + 19)
                conclude(6)

            for s in range(1, NSUB):
                split_inputs(s)
                lo(FIRST[s] + 1)
                if s in SWIGLUS:
                    swiglu(s)
                elif s == 3:
                    attention()
                else:
                    hgrn()

        @block.tensor
        def _(pe):
            def three(dst, xh, xl, wh, wl, first, final, weights_move=True):
                for n, (a, w) in enumerate(((xh, wh), (xh, wl), (xl, wh))):
                    lhsT, rhs = (a, w) if weights_move else (w, a)
                    done = pe.matmul(dst, lhsT, rhs, start=first and n == 0, stop=final and n == 2, skip_group_check=True)
                return done

            def columns_by_token(unit, g, banks, n=BANK, lap=0, ready=None, inputs=None):
                slot = unit % RING
                pe.wait_ge(w_lo, unit + 1 + RING * lap)
                for t in range(NT):
                    if inputs is not None:
                        pe.wait_ge(h_lo, 4 * inputs + 2 * t + g + 1)
                    for k in range(4):
                        kt = 4 * g + k
                        tok_cols = slice(t * P, (t + 1) * P)
                        done = three(ps[:, banks[t], 0:n], hhi[:, kt, tok_cols], hlo[:, kt, tok_cols],
                                     whi[:, slot, k * n:(k + 1) * n], wlo[:, slot, k * n:(k + 1) * n],
                                     g == 0 and k == 0, g == 1 and k == 3)
                    if g == 1 and t == 0:
                        done.then_inc(ready, 1)
                done.then_inc(w_used, 1)

            def columns_by_feature(unit, g, b):
                slot = unit % RING
                pe.wait_ge(w_lo, unit + 1)
                for ct in range(4):
                    dst = psf[:, b * BANK + ct * TOK:b * BANK + (ct + 1) * TOK]
                    for k in range(4):
                        kt, cols = 4 * g + k, slice(k * BANK + ct * P, k * BANK + (ct + 1) * P)
                        done = three(dst, hhi[:, kt, :], hlo[:, kt, :], whi[:, slot, cols], wlo[:, slot, cols],
                                     g == 0 and k == 0 and ct % 2 == 0, g == 1 and k == 3, weights_move=False)
                done.then_inc(w_used, 1)

            def down_rows(unit, hi_of, lo_of, first, final, lap=0, before=None, end=None):
                slot = unit % RING
                pe.wait_ge(w_lo, unit + 1 + RING * lap)
                for t in range(NT):
                    if before:
                        before(t)
                    for h in range(2):
                        for k in range(2):
                            cols = slice(k * D + h * BANK, k * D + (h + 1) * BANK)
                            done = three(bank(2 * t + h), hi_of(k, t), lo_of(k, t), whi[:, slot, cols], wlo[:, slot, cols],
                                         first and k == 0, final and k == 1)
                    if final and t == 0:
                        done.then_inc(y_ready, 1)
                done.then_inc(w_used, 1)

            def transposes(blocks, b, signal):
                for n, a in enumerate(blocks):
                    done = pe.transpose(ps[:, b, n * P:(n + 1) * P], a, ident)
                done.then_inc(signal, 1)

            def sum_columns(s):
                if s == 0:
                    pe.wait_ge(w_lo, KT)
                else:
                    pe.wait_ge(a_used, pieces_until(s, 0))
                    pe.wait_ge(cols_set, s)
                for j in range(16):
                    done = pe.matmul(ps[:, COL_BANK, j:j + 1], ada_acc[:, s % 2, j * P:(j + 1) * P], ones[:, 0:1],
                                     start=True, stop=True)
                done.then_inc(cols_sum, 1)

            def sum_gate(s):
                pe.wait_ge(a_used, pieces_until(s, 2) if s else KT)
                for h in range(2):
                    done = pe.matmul(bank(gate_bank(s) + h), ones[:, :], ada_acc[:, s % 2, 2 * D + h * BANK:2 * D + (h + 1) * BANK],
                                     start=True, stop=True)
                done.then_inc(gate_sum, 1)

            def transpose_inputs(s):
                for t in range(NT):
                    if s == 0:
                        pe.wait_ge(x_land, 32)
                        pe.wait_ge(vec_set, 1)
                    elif s == 1:
                        pe.wait_ge(x_new, t + 1)
                    else:
                        pe.wait_ge(h_src, 2 * (s - 2) + t + 1)
                    src = xs if s < 2 else xn
                    for g in range(2):
                        transposes([src[:, t, (4 * g + k) * P:(4 * g + k + 1) * P] for k in range(4)], 2 * t + g, h_tr)

            def output_product(s, unit, mixed_ready, k0=0):
                for j in range(4):
                    k_j = (k0 + 2 * j) % KT

                    def before(t):
                        if (j, t) in mixed_ready:
                            pe.wait_ge(mix_lo, mixed_ready[j, t])
                    down_rows(unit + j, lambda k, t: hhi[:, k_j + k, t * P:(t + 1) * P],
                              lambda k, t: hlo[:, k_j + k, t * P:(t + 1) * P], j == 0, j == 3, before=before)
                if s < NSUB - 1:
                    sum_columns(s + 1)

            def swiglu(s):
                m = SWIGLUS.index(s) * NCH
                U = FIRST[s]

                def gate_up(unit, g, i, lap=0, first_chunk=False):
                    if g == 0 and not first_chunk:
                        pe.wait_ge(act_ready, 2 * (m + i))
                    columns_by_token(unit, g, (4, 5), lap=lap, ready=gu_ready, inputs=s if first_chunk else None)

                def turn(i):
                    pe.wait_ge(act_ready, 2 * (m + i + 1))
                    pe.wait_ge(alo_ready, m + i)
                    for k in range(2):
                        for t in range(NT):
                            done = pe.transpose(ps[:, 6, k * TOK + t * P:k * TOK + (t + 1) * P],
                                                act[:, t, k * P:(k + 1) * P], ident)
                    done.then_inc(tr_ready, 1)

                def down(unit, i, lap=0, first=False, final=False, before=None):
                    pe.wait_ge(alo_ready, m + i + 1)
                    a_hi, a_lo = split_places(final)
                    down_rows(unit, lambda k, t: a_hi[:, k, t * P:(t + 1) * P], lambda k, t: a_lo[:, k, t * P:(t + 1) * P],
                              first, final, lap=lap, before=before)

                def body(first, i, lap=0, first_down=False, before=None):
                    gate_up(first, 0, i, lap)
                    turn(i - 1)
                    gate_up(first + 1, 1, i, lap)
                    down(first + 2, i - 1, lap, first=first_down, before=before)

                gate_up(U, 0, 0, first_chunk=True)
                gate_up(U + 1, 1, 0, first_chunk=True)
                if s not in LATE_GATES:
                    pe.wait_ge(gate_set, s + 1)
                body(U + 2, 1, first_down=True)
                if s == 1:
                    pe.wait_ge(toe_fill, 2)
                    pe.wait_ge(cols_set, 2)
                    for h in range(HEADS):
                        if h >= 2:
                            pe.wait_ge(toe_rows, h - 1)
                        pe.matmul(ps[:, 6 + h % 2, 0:TOE], big[0:BUCKETS + 1, 2560 + h * P:2560 + (h + 1) * P],
                                  big[0:BUCKETS + 1, 2048:2048 + TOE], start=True, stop=True).then_inc(toe_mm, 1)
                    pe.wait_ge(toe_rows, HEADS)
                with pe.Fori(2, NCH - 1) as i:
                    body(U + 5, i, i - 2)
                def last_turn(t):
                    if t == 1:
                        turn(NCH - 1)

                body(U + 3 * (NCH - 1) - 1, NCH - 1, before=last_turn)
                if s in LATE_GATES:
                    sum_gate(s)
                down(U + UNITS[s] - 1, NCH - 1, final=True)
                if s in LATE_GATES:
                    pe.wait_ge(gate_set, s + 1)
                if s < NSUB - 1:
                    sum_columns(s + 1)

            def attention():
                U = FIRST[3]
                with pe.Fori(0, 2) as i:
                    for b in range(3):
                        for g in range(2):
                            columns_by_token(U + 2 * b + g, g, (2 * b, 2 * b + 1), lap=2 * i, ready=blk_ready,
                                             inputs=3 if b == 0 else None)
                    pe.wait_ge(qk_out, 4 * i + 4)
                    pe.wait_ge(v_out, 2 * i + 2)
                pe.wait_ge(gate_set, 4)
                for t in range(NT):
                    for g in range(2):
                        for b in range(2):
                            transposes([qkv[:, t, b * D + (4 * g + h) * P:b * D + (4 * g + h + 1) * P] for h in range(4)],
                                       4 * t + 2 * g + b, qk_tr)

                def dots(i):
                    t, h = divmod(i, HEADS)
                    keys = P * (t + 1)
                    if i == 0:
                        pe.wait_ge(qT3, 4)
                        pe.wait_ge(kT3, 4)
                    if i >= 2:
                        pe.wait_ge(sm_ready, i - 1)
                    for c in range(2):
                        rows = slice(64 * c, 64 * c + 64)
                        done = pe.matmul(ps[:, 2 * (i % 2) + c, 0:keys], qT[rows, h, t * P:(t + 1) * P], kT[rows, h, 0:keys],
                                         start=True, stop=True)
                    done.then_inc(dot_mm, 1)

                def turn(i):
                    pe.wait_ge(a_ready, i + 1)
                    if i >= 2:
                        pe.wait_ge(aT_out, i - 1)
                    for g in range(i // HEADS + 1):
                        done = pe.transpose(ps[:, 4 + i % 2, g * P:(g + 1) * P], soft[:, i % 2, 0, g * P:(g + 1) * P], ident)
                    done.then_inc(a_tr, 1)

                def values(i):
                    t, h = divmod(i, HEADS)
                    pe.wait_ge(aT_out, i + 1)
                    if i == HEADS:
                        pe.wait_ge(o_done, 2 + 1)
                    for g in range(t + 1):
                        done = pe.matmul(psf[:, 6 * BANK + h * P:6 * BANK + (h + 1) * P], weightsT[:, i % 2, g * P:(g + 1) * P],
                                         qkv[:, g, 2 * D + h * P:2 * D + (h + 1) * P], start=g == 0, stop=g == t)
                    done.then_inc(av_mm, 1)

                dots(0)
                for i in range(2 * HEADS):
                    if i + 1 < 2 * HEADS:
                        dots(i + 1)
                    if i:
                        turn(i - 1)
                    if i >= 2:
                        values(i - 2)
                turn(2 * HEADS - 1)
                values(2 * HEADS - 2)
                values(2 * HEADS - 1)
                for t in range(NT):
                    pe.wait_ge(o_done, 2 + t + 1)
                    for g in range(2):
                        transposes([qkv[:, t, (4 * g + k) * P:(4 * g + k + 1) * P] for k in range(4)], 2 * t + g, o_tr)
                output_product(3, U + 12, {(0, 0): 4, (2, 0): 5, (0, 1): 6, (2, 1): 7})

            def hgrn():
                U = FIRST[6]
                for g in range(2):
                    pe.wait_ge(h_lo, 4 * 6 + 3 + g)
                    columns_by_feature(U + g, g, 0)
                for g in range(2):
                    columns_by_feature(U + 2 + g, g, 2)
                for b in range(2):
                    pe.wait_ge(f_taken, b + 1)
                    for g in range(2):
                        columns_by_feature(U + 4 + 2 * b + g, g, 2 * b)

                def scores(level):
                    for t in range(NT if level <= len(LEVELS) else 1):
                        if level:
                            pe.wait_ge(lv_copy, 2 * level - 1 + t)
                        cols = slice(t * P, (t + 1) * P)
                        for h in range(HEADS):
                            dst = psf[:, (4 + 2 * t) * BANK + h * P:(4 + 2 * t) * BANK + (h + 1) * P]
                            if level == 0:
                                lhsT, rhs = h_k[:, h, cols], h_q[:, h, cols]
                            elif level <= len(LEVELS):
                                lhsT = rhs = decayed(level)[:, h, cols]
                            else:
                                lhsT, rhs = decayed(level)[:, h, 0:P], decayed(level)[:, h, P:TOK]
                            done = pe.matmul(dst, lhsT, rhs, start=True, stop=True)
                        done.then_inc(lv_mm, 1)

                for level in range(len(LEVELS) + 2):
                    if level <= 7:
                        b, g = divmod(level, 2)
                        if g == 0:
                            if b < 2:
                                pe.wait_ge(q_copied, b + 1)
                            else:
                                pe.wait_ge(vg_out, 2 * (b - 1))
                        columns_by_token(U + 8 + level, g, (2 * (b % 2), 2 * (b % 2) + 1), ready=blk_ready)
                    if level == 0:
                        pe.wait_ge(k_ready, 2)
                        pe.wait_ge(q_copied, 2)
                        pe.wait_ge(gate_set, 7)
                    else:
                        pe.wait_ge(lv_mul, level)
                    scores(level)
                pe.wait_ge(lv_copy, 2 * (len(LEVELS) + 1) + 1)
                pe.wait_ge(vg_out, 8)
                for t in range(NT):
                    for h in range(HEADS):
                        cols = slice(h * P, (h + 1) * P)
                        dst = psf[:, 2 * t * BANK + h * P:2 * t * BANK + (h + 1) * P]
                        done = pe.matmul(dst, scoresT[:, HEADS * t + h, :], h_v[:, t, cols], start=True, stop=t == 0)
                        if t:
                            done = pe.matmul(dst, scoresT[:, 2 * HEADS + h, :], h_v[:, 0, cols], start=False, stop=True)
                    done.then_inc(pv_mm, 1)
                for t in range(NT):
                    pe.wait_ge(o_done, 4 + t + 1)
                    for g in range(2):
                        transposes([h_o[:, t, (4 * g + k) * P:(4 * g + k + 1) * P] for k in range(4)], 2 * t + g, o_tr)
                output_product(6, U + 16, {(0, 0): 8, (2, 0): 9, (0, 1): 10, (2, 1): 11})

            pe.wait_ge(const_land, 16)
            pe.wait_ge(vec_land, 208)
            pe.transpose(ps[:, 0, 0:NVEC], big[0:NVEC, 0:P], kc[0:NVEC, C_ID:C_ID + NVEC]).then_inc(vec_tr, 1)
            pe.wait_ge(ones_set, 3)
            transpose_inputs(0)
            sum_columns(0)
            U = FIRST[0]
            tok = big[:, 2048:2048 + NT * TOKC].rearrange("p (t n) -> p t n", t=NT)
            L = big[:, 3920:5968].rearrange("p (h k) -> p h k", h=HEADS)
            PT = big[:, 5968:8016].rearrange("p (g n) -> p g n", g=2)
            xfl = xn[:, :, :].rearrange("p t n -> p (t n)")
            kk = big[:, 8592:8848].rearrange("p (t n) -> p t n", t=NT)
            ki4 = big[:, 8848:9104].rearrange("p (t n) -> p t n", t=NT)
            for g in range(2):
                columns_by_token(U + g, g, (4, 5), ready=blk_ready, inputs=0)
            for g in range(2):
                columns_by_token(U + 2 + g, g, (6, 7), n=TOKC - BANK, ready=blk_ready)
            for g in range(2):
                columns_by_feature(U + 4 + g, g, 0)
            pe.wait_ge(rope_done, 1)
            pe.wait_ge(q_out, 2)
            sources = [lambda t, j=j: tok[:, t, j * P:(j + 1) * P] for j in range(4)]
            sources += [lambda t: kk[:, t, :]] + [lambda t, j=j: tok[:, t, QIO + j * P:QIO + (j + 1) * P] for j in range(2)]
            sources += [lambda t: ki4[:, t, :]]
            for n, src in enumerate(sources):
                for t in range(NT):
                    done = pe.transpose(psf[:, 4 * BANK + n * TOK + t * P:4 * BANK + n * TOK + (t + 1) * P], src(t), ident)
                if n in (3, 7):
                    done.then_inc(qk_tr, 1)
            columns_by_feature(U + 6, 0, 2)

            def index_products(t):
                keys = P * (t + 1)
                for j in range(2):
                    for r in range(4):
                        rows = slice(32 * r, 32 * r + 32)
                        done = pe.matmul(ps[:, 4 + r, j * keys:(j + 1) * keys],
                                         xfl[rows, D + TOK * (1 + j) + t * P:D + TOK * (1 + j) + (t + 1) * P],
                                         xfl[rows, D + 3 * TOK:D + 3 * TOK + keys], start=True, stop=True)
                done.then_inc(idx_mm, 1)

            pe.wait_ge(qT_out, 1)
            pe.wait_ge(kT_out, 1)
            index_products(0)
            columns_by_feature(U + 7, 1, 2)
            pe.wait_ge(relu_done, 1)
            index_products(1)
            pe.wait_ge(hc_out, 1)
            columns_by_feature(U + 8, 0, 0)
            columns_by_feature(U + 9, 1, 0)

            def logit_products(t):
                keys = P * (t + 1)
                for j in range(4):
                    for r in range(2):
                        rows = slice(64 * r, 64 * r + 64)
                        at_col = (4 + 2 * r) * BANK + j * TOK
                        done = pe.matmul(psf[:, at_col:at_col + keys], xfl[rows, j * TOK + t * P:j * TOK + (t + 1) * P],
                                         xfl[rows, D:D + keys], start=True, stop=True)
                done.then_inc(att_mm, 1)

            def turn_weights(t):
                pe.wait_ge(exp_done, t + 1)
                for g in range(t + 1):
                    for h in range(HEADS):
                        done = pe.transpose(psf[:, (4 + 2 * g) * BANK + h * P:(4 + 2 * g) * BANK + (h + 1) * P],
                                            L[:, h, g * P:(g + 1) * P], ident)
                done.then_inc(p_tr, 1)

            def attend(t):
                pe.wait_ge(pt_s, t + 1)
                if t:
                    pe.wait_ge(pt_v, 1)
                for h in range(HEADS):
                    for g in range(t + 1):
                        done = pe.matmul(ps[:, 2 + t, h * 64:(h + 1) * 64], PT[:, g, h * P:(h + 1) * P],
                                         tok[:, g, VO:VO + 64], start=g == 0, stop=g == t)
                done.then_inc(pv_mm, 1)

            pe.wait_ge(relu_done, 2)
            logit_products(0)
            pe.wait_ge(conv_u, 1)
            sum_gate(0)
            turn_weights(0)
            pe.wait_ge(pt_s, 1)
            logit_products(1)
            pe.wait_ge(gate_set, 1)
            attend(0)
            turn_weights(1)
            pe.wait_ge(conv_sq, 1)
            for t in range(NT):
                for ct in range(4):
                    done = pe.matmul(ps[:, 0, 8 * t + 2 * ct:8 * t + 2 * ct + 2], hf[:, ct, t * P:(t + 1) * P],
                                     kc[:, C_HALF:C_HALF + 2], start=True, stop=True)
            done.then_inc(group_mm, 1)
            attend(1)
            pe.wait_ge(root, 1)
            for t in range(NT):
                done = pe.transpose(ps[0:8, 1, t * P:(t + 1) * P], st[:, 40 + 8 * t:48 + 8 * t], ident)
            done.then_inc(group_tr, 1)
            pe.wait_ge(group_out, 1)
            pe.wait_ge(spread_land, 16)
            for ct in range(4):
                done = pe.matmul(psf[:, ct * TOK:(ct + 1) * TOK], gate[0:8, 1, ct * P:(ct + 1) * P], act[0:8, 0, 0:TOK],
                                 start=True, stop=True)
            done.then_inc(spread_mm, 1)
            for t in range(NT):
                pe.wait_ge(o_done, t + 1)
                transposes([big[:, 3920 + BANK * t + j * P:3920 + BANK * t + (j + 1) * P] for j in range(4)], 4 + t, o_tr)
            pe.wait_ge(mix_f, 3)
            output_product(0, U + 10, {(0, 0): 1, (2, 0): 2, (2, 1): 3}, 4)

            for s in range(1, NSUB):
                transpose_inputs(s)
                if s not in LATE_GATES:
                    sum_gate(s)
                if s in SWIGLUS:
                    swiglu(s)
                elif s == 3:
                    attention()
                else:
                    hgrn()


INPUTS = (
    "x c w_ada b_ada w_in conv_w attn_norm_g conv_norm_g w_out ln1_g ln1_b w_gate w_up w_down ln2_g ln2_b c_2 ada_w_2 "
    "ada_b_2 norm_g_2 ffn_w_in_2 ffn_w_down_2 attn_w_qkv_2 attn_w_o_2 attn_q_gain_2 attn_k_gain_2 attn_lambda_2 "
    "attn_subln_gain_2 rel_bias_2 hgrn_w_in_2 hgrn_w_o_2 hgrn_out_gain_2 hgrn_lb_logits_2"
).split()


def kernel(**inputs):
    import concourse.bacc as bacc
    from concourse.bass_utils import run_bass_kernel_spmd

    nc = bacc.Bacc("TRN2", target_bir_lowering=False, num_devices=1)
    arrays, args = {}, []
    for name in INPUTS:
        a = np.ascontiguousarray(inputs[name])
        arrays[f"in_{name}"] = a
        args.append(nc.dram_tensor(f"in_{name}", a.shape, mybir.dt.from_np(a.dtype), kind="ExternalInput").ap())
    args.append(nc.dram_tensor("out_x", (1, TOK, D), F32, kind="ExternalOutput").ap())
    two_blocks(nc, *args)
    r = run_bass_kernel_spmd(nc, [arrays], core_ids=[0])
    return r.results[0]["out_x"]
```
